# Optimizing a Trainium2 kernel written in Bass

```python
import jax, jax.numpy as jnp
from jax import lax
import numpy as np
import jax
import jax.numpy as jnp

D_MODEL = 1024
BATCH = 1
SEQ = 512
DEPTH = 2

N_META = 16
H_A = 4
QK_NOPE = 128
QK_ROPE = 64
V_DIM = 128
Q_LORA = 256
KV_LORA = 128
ROPE_THETA = 10000.0
Q_BLOCK = 128
H_B = 8
N_B = 64
RW = H_B * N_B
DECAY_LORA = 64
AAA_LORA = 64
GATE_LORA = 128
VRES_LORA = 32
RWKV_GN_EPS = 64e-5
MIX = H_A * V_DIM + RW
MLA_COLS = Q_LORA + KV_LORA + QK_ROPE
RWKV_COLS = 3 * RW + 2 * DECAY_LORA + 2 * AAA_LORA + GATE_LORA
IN_COLS = MLA_COLS + RWKV_COLS
N_GROUPS = 4
EXPERTS_PER_GROUP = 8
N_EXPERTS = N_GROUPS * EXPERTS_PER_GROUP
TOP_K = 2
E_HID = 256
MOE_BLOCK = 128
DN_ALPHA = (2 * DEPTH) ** 0.25
DN_BETA = (8 * DEPTH) ** -0.25
LN_EPS = 1e-5
RMS_EPS = 1e-6


def _split(t, sizes):
    return jnp.split(t, np.cumsum(sizes)[:-1].tolist(), axis=-1)

def _layer_norm(x, g, b):
    xf = x.astype(jnp.float32)
    mu = jnp.mean(xf, -1, keepdims=True)
    var = jnp.mean(jnp.square(xf - mu), -1, keepdims=True)
    return ((xf - mu) * lax.rsqrt(var + LN_EPS) * g + b).astype(x.dtype)

def _rms_norm(x, g):
    xf = x.astype(jnp.float32)
    return (xf * lax.rsqrt(jnp.mean(xf * xf, -1, keepdims=True) + RMS_EPS) * g).astype(x.dtype)

def _rope(t, cos, sin):
    half = t.shape[-1] // 2
    t1, t2 = t[..., :half], t[..., half:]
    return jnp.concatenate([t1 * cos - t2 * sin, t2 * cos + t1 * sin], -1).astype(t.dtype)

def _centred_shift(p, mu_prev, mu_next):
    prev = jnp.pad(p[:, :-1], ((0, 0), (1, 0), (0, 0)))
    nxt = jnp.pad(p[:, 1:], ((0, 0), (0, 1), (0, 0)))
    return p + mu_prev * (prev - p) + mu_next * (nxt - p)

def _mla(c_q, c_kv, k_pe, cos, sin, q_norm, kv_norm, w_uq, w_ukv, out_norm):
    B, L, _ = c_q.shape
    q = (_rms_norm(c_q, q_norm) @ w_uq).reshape(B, L, H_A, QK_NOPE + QK_ROPE)
    q_nope = q[..., :QK_NOPE]
    q_pe = _rope(q[..., QK_NOPE:], cos[:, :, None, :], sin[:, :, None, :])
    kv = (_rms_norm(c_kv, kv_norm) @ w_ukv).reshape(B, L, H_A, QK_NOPE + V_DIM)
    k_nope, v = kv[..., :QK_NOPE], kv[..., QK_NOPE:]
    k_pe = _rope(k_pe, cos, sin)
    scale = (QK_NOPE + QK_ROPE) ** -0.5

    def attend(blk):
        qn, qp = blk
        s = jnp.einsum('bqhd,bkhd->bhqk', qn, k_nope) + jnp.einsum('bqhd,bkd->bhqk', qp, k_pe)
        p = jax.nn.softmax(s.astype(jnp.float32) * scale, axis=-1).astype(v.dtype)
        return jnp.einsum('bhqk,bkhd->bqhd', p, v)

    out_meta = attend((q_nope[:, :N_META], q_pe[:, :N_META]))
    n_blk = (L - N_META) // Q_BLOCK

    def to_blocks(t):
        return jnp.moveaxis(t[:, N_META:].reshape(B, n_blk, Q_BLOCK, H_A, t.shape[-1]), 1, 0)

    out_real = lax.map(attend, (to_blocks(q_nope), to_blocks(q_pe)))
    out_real = jnp.moveaxis(out_real, 0, 1).reshape(B, L - N_META, H_A, V_DIM)
    out = jnp.concatenate([out_meta, out_real], axis=1)
    out = _rms_norm(out, out_norm.reshape(H_A, V_DIM))
    return out.reshape(B, L, H_A * V_DIM)

def _wkv_scan(r, decay, k, v, kk, a, reverse):
    B = r.shape[0]

    def step(S, inp):
        r_t, w_t, k_t, v_t, kk_t, b_t = inp
        sa = jnp.einsum('bhvk,bhk->bhv', S, kk_t)
        S = S * w_t[:, :, None, :] - sa[..., None] * b_t[:, :, None, :] + v_t[..., None] * k_t[:, :, None, :]
        return S, jnp.einsum('bhvk,bhk->bhv', S, r_t)

    xs = tuple(jnp.moveaxis(t, 1, 0) for t in (r, decay, k, v, kk, kk * a))
    S0 = jnp.zeros((B, H_B, N_B, N_B), jnp.float32)
    _, ys = lax.scan(step, S0, xs, reverse=reverse)
    return jnp.moveaxis(ys, 0, 1)

def _rwkv_bidir(u, v_first, vres, w0, w2, a0, a2, g2, k_k, k_a, r_k, gn_g, gn_b):
    dt = u.dtype
    u = u.astype(jnp.float32)
    B, L, _ = u.shape
    r, k, v, wd_f, wd_b, ad_f, ad_b, gd = _split(
        u, [RW, RW, RW, DECAY_LORA, DECAY_LORA, AAA_LORA, AAA_LORA, GATE_LORA])
    if vres is None:
        v_first = v
    else:
        v0, v1, v2 = vres
        v = v + (v_first - v) * jax.nn.sigmoid(v0 + (v @ v1) @ v2)
    g = jax.nn.sigmoid(gd) @ g2

    def heads(t):
        return t.reshape(B, L, H_B, N_B)

    kk = heads(k * k_k)
    kk = kk * lax.rsqrt(jnp.sum(kk * kk, -1, keepdims=True) + 1e-12)
    rh, vh = heads(r), heads(v)

    def direction(d, wd, ad, reverse):
        wl = w0[d] + jnp.tanh(wd) @ w2[d]
        decay = jnp.exp(-jnp.exp(-jax.nn.softplus(-wl) - 0.5))
        a = jax.nn.sigmoid(a0[d] + ad @ a2[d])
        kd = heads(k * (1.0 + (a - 1.0) * k_a))
        y = _wkv_scan(rh, heads(decay), kd, vh, kk, heads(a), reverse)
        bonus = jnp.sum(rh * kd * r_k, -1, keepdims=True) * vh
        return y, bonus

    y_f, bonus_f = direction(0, wd_f, ad_f, False)
    y_b, bonus_b = direction(1, wd_b, ad_b, True)
    y = y_f + y_b
    mu = jnp.mean(y, -1, keepdims=True)
    var = jnp.mean(jnp.square(y - mu), -1, keepdims=True)
    yn = ((y - mu) * lax.rsqrt(var + RWKV_GN_EPS)).reshape(B, L, RW) * gn_g + gn_b
    out = (yn + (bonus_f + bonus_b).reshape(B, L, RW)) * g
    return out.astype(dt), v_first

def _hier_moe(h, w_group, b_group, w_expert, b_expert, w1, w3, w2):
    T, D = h.shape
    g_prob = jax.nn.softmax((h @ w_group).astype(jnp.float32) + b_group, axis=-1)
    g_top_p, g_top = lax.top_k(g_prob, 1)
    e_logits = ((h @ w_expert).astype(jnp.float32) + b_expert).reshape(T, N_GROUPS, EXPERTS_PER_GROUP)
    e_logits = jnp.take_along_axis(e_logits, g_top[:, :, None], axis=1)[:, 0]
    e_top_p, e_top = lax.top_k(jax.nn.softmax(e_logits, axis=-1), TOP_K)
    gate = (g_top_p * e_top_p).reshape(-1)
    flat_e = (g_top * EXPERTS_PER_GROUP + e_top).reshape(-1)
    flat_tok = jnp.repeat(jnp.arange(T, dtype=jnp.int32), TOP_K)
    order = jnp.argsort(flat_e)
    se = flat_e[order]
    counts = jnp.bincount(flat_e, length=N_EXPERTS)
    starts = jnp.cumsum(counts) - counts
    padded = (counts + MOE_BLOCK - 1) // MOE_BLOCK * MOE_BLOCK
    pends = jnp.cumsum(padded)
    dest = (pends - padded)[se] + jnp.arange(T * TOP_K) - starts[se]
    n_rows = (T * TOP_K + N_EXPERTS * (MOE_BLOCK - 1) + MOE_BLOCK - 1) // MOE_BLOCK * MOE_BLOCK
    n_blocks = n_rows // MOE_BLOCK
    row_tok = jnp.zeros((n_rows,), jnp.int32).at[dest].set(flat_tok[order])
    row_gate = jnp.zeros((n_rows,), jnp.float32).at[dest].set(gate[order])
    block_e = jnp.clip(jnp.searchsorted(pends, jnp.arange(n_blocks) * MOE_BLOCK, side='right'),
                       0, N_EXPERTS - 1)
    xb = h[row_tok].reshape(n_blocks, MOE_BLOCK, D)

    def expert_block(args):
        xe, e = args
        return (jax.nn.silu(xe @ w1[e]) * (xe @ w3[e])) @ w2[e]

    yb = lax.map(expert_block, (xb, block_e)).reshape(n_rows, D)
    y = jnp.zeros((T, D), jnp.float32).at[row_tok].add(yb.astype(jnp.float32) * row_gate[:, None])
    return y.astype(h.dtype)

def first_inputs(seed: int = 0) -> dict:
    key = jax.random.key(seed)
    ks = iter(jax.random.split(key, 48))

    def nrm(shape, s):
        return jax.random.normal(next(ks), shape, jnp.float32) * s

    def uni(shape, lo, hi):
        return jax.random.uniform(next(ks), shape, jnp.float32, lo, hi)

    D = D_MODEL
    return {
        'x': nrm((BATCH, SEQ, D), 1.0),
        'positions': jnp.tile(jnp.arange(SEQ, dtype=jnp.int32)[None], (BATCH, 1)),
        'meta_tokens': nrm((N_META, D), 1.0),
        'emb_ln_g': 1.0 + nrm((D,), 0.02),
        'emb_ln_b': nrm((D,), 0.02),
        'w_in': nrm((DEPTH, D, IN_COLS), D ** -0.5),
        'mla_q_norm': 1.0 + nrm((DEPTH, Q_LORA), 0.02),
        'mla_kv_norm': 1.0 + nrm((DEPTH, KV_LORA), 0.02),
        'mla_w_uq': nrm((DEPTH, Q_LORA, H_A * (QK_NOPE + QK_ROPE)), Q_LORA ** -0.5),
        'mla_w_ukv': nrm((DEPTH, KV_LORA, H_A * (QK_NOPE + V_DIM)), KV_LORA ** -0.5),
        'mla_out_norm': 1.0 + nrm((DEPTH, H_A * V_DIM), 0.02),
        'rwkv_mu_prev': uni((DEPTH, RWKV_COLS), 0.0, 0.5),
        'rwkv_mu_next': uni((DEPTH, RWKV_COLS), 0.0, 0.5),
        'rwkv_w0': uni((DEPTH, 2, RW), -4.0, 0.0),
        'rwkv_w2': nrm((DEPTH, 2, DECAY_LORA, RW), 0.1),
        'rwkv_a0': nrm((DEPTH, 2, RW), 0.3),
        'rwkv_a2': nrm((DEPTH, 2, AAA_LORA, RW), 0.1),
        'rwkv_g2': nrm((DEPTH, GATE_LORA, RW), GATE_LORA ** -0.5),
        'rwkv_k_k': 0.85 + nrm((DEPTH, RW), 0.05),
        'rwkv_k_a': 1.0 + nrm((DEPTH, RW), 0.05),
        'rwkv_r_k': nrm((DEPTH, H_B, N_B), 0.1),
        'rwkv_gn_g': 1.0 + nrm((DEPTH, RW), 0.02),
        'rwkv_gn_b': nrm((DEPTH, RW), 0.02),
        'rwkv_v0': nrm((DEPTH - 1, RW), 0.3),
        'rwkv_v1': nrm((DEPTH - 1, RW, VRES_LORA), RW ** -0.5),
        'rwkv_v2': nrm((DEPTH - 1, VRES_LORA, RW), 0.5 * VRES_LORA ** -0.5),
        'w_out': nrm((DEPTH, MIX, D), DN_BETA * MIX ** -0.5),
        'ln1_g': 1.0 + nrm((DEPTH, D), 0.02),
        'ln1_b': nrm((DEPTH, D), 0.02),
        'moe_w_group': nrm((DEPTH, D, N_GROUPS), D ** -0.5),
        'moe_b_group': nrm((DEPTH, N_GROUPS), 0.01),
        'moe_w_expert': nrm((DEPTH, D, N_EXPERTS), D ** -0.5),
        'moe_b_expert': nrm((DEPTH, N_EXPERTS), 0.01),
        'moe_w1': nrm((DEPTH, N_EXPERTS, D, E_HID), D ** -0.5),
        'moe_w3': nrm((DEPTH, N_EXPERTS, D, E_HID), D ** -0.5),
        'moe_w2': nrm((DEPTH, N_EXPERTS, E_HID, D), DN_BETA * E_HID ** -0.5),
        'ln2_g': 1.0 + nrm((DEPTH, D), 0.02),
        'ln2_b': nrm((DEPTH, D), 0.02),
    }

def first_block(x, positions, meta_tokens, emb_ln_g, emb_ln_b, w_in, mla_q_norm, mla_kv_norm,
              mla_w_uq, mla_w_ukv, mla_out_norm, rwkv_mu_prev, rwkv_mu_next, rwkv_w0, rwkv_w2,
              rwkv_a0, rwkv_a2, rwkv_g2, rwkv_k_k, rwkv_k_a, rwkv_r_k, rwkv_gn_g, rwkv_gn_b,
              rwkv_v0, rwkv_v1, rwkv_v2, w_out, ln1_g, ln1_b, moe_w_group, moe_b_group,
              moe_w_expert, moe_b_expert, moe_w1, moe_w3, moe_w2, ln2_g, ln2_b):
    B = x.shape[0]
    meta = jnp.broadcast_to(meta_tokens.astype(x.dtype)[None], (B, N_META, D_MODEL))
    h = _layer_norm(jnp.concatenate([meta, x], axis=1), emb_ln_g, emb_ln_b)
    L = h.shape[1]
    pos = jnp.concatenate([jnp.broadcast_to(jnp.arange(N_META, dtype=jnp.int32), (B, N_META)),
                           positions + N_META], axis=1)
    inv_freq = ROPE_THETA ** (-jnp.arange(0, QK_ROPE, 2, dtype=jnp.float32) / QK_ROPE)
    ang = pos.astype(jnp.float32)[..., None] * inv_freq
    cos, sin = jnp.cos(ang), jnp.sin(ang)
    v_first = None
    for li in range(DEPTH):
        proj = h @ w_in[li]
        c_q, c_kv, k_pe, rw = _split(proj, [Q_LORA, KV_LORA, QK_ROPE, RWKV_COLS])
        y_att = _mla(c_q, c_kv, k_pe, cos, sin, mla_q_norm[li], mla_kv_norm[li],
                     mla_w_uq[li], mla_w_ukv[li], mla_out_norm[li])
        u = _centred_shift(rw, rwkv_mu_prev[li], rwkv_mu_next[li])
        vres = None if li == 0 else (rwkv_v0[li - 1], rwkv_v1[li - 1], rwkv_v2[li - 1])
        y_rwkv, v_first = _rwkv_bidir(u, v_first, vres, rwkv_w0[li], rwkv_w2[li], rwkv_a0[li],
                                      rwkv_a2[li], rwkv_g2[li], rwkv_k_k[li], rwkv_k_a[li],
                                      rwkv_r_k[li], rwkv_gn_g[li], rwkv_gn_b[li])
        mixed = jnp.concatenate([y_att, y_rwkv], axis=-1) @ w_out[li]
        h = _layer_norm(DN_ALPHA * h + mixed, ln1_g[li], ln1_b[li])
        ff = _hier_moe(h.reshape(B * L, D_MODEL), moe_w_group[li], moe_b_group[li],
                       moe_w_expert[li], moe_b_expert[li], moe_w1[li], moe_w3[li],
                       moe_w2[li]).reshape(B, L, D_MODEL)
        h = _layer_norm(DN_ALPHA * h + ff, ln2_g[li], ln2_b[li])
    return h[:, N_META:]


DEPTH_2 = 1

CTX_LEN = 256
GRID_W = 64
HEAD_DIM = 64
BRANCH_WIDTH = 512
N_BRANCH = 3
A_HEADS = 8
A_KV_HEADS = 2
WINDOW = 128
B_HEADS = 8
B_KV_HEADS = 2
C_HEADS = 4
C_DK = 128
C_DV = 128
CHUNK = 64
BLOCK = 128
D_FF = 2816
CONV_W = 3
AXIS_ROPE_DIM = HEAD_DIM // 2
N_MOD = 6
EPS = 1e-6
NEG_BIG = -1e30
PROJ_SIZES = (A_HEADS * HEAD_DIM, A_KV_HEADS * HEAD_DIM, A_KV_HEADS * HEAD_DIM,
              B_HEADS * HEAD_DIM, B_KV_HEADS * HEAD_DIM, B_KV_HEADS * HEAD_DIM,
              C_HEADS * C_DK, C_HEADS * C_DK, C_HEADS * C_DK, C_HEADS * C_DV, C_HEADS * C_DV,
              N_BRANCH * D_MODEL)
PROJ_WIDTH = sum(PROJ_SIZES)


def rms_norm(t, g):
    tf = t.astype(jnp.float32)
    y = tf * lax.rsqrt(jnp.mean(tf * tf, axis=-1, keepdims=True) + EPS)
    return (y * g.astype(jnp.float32)).astype(t.dtype)

def axial_rope(n):
    rows = n // GRID_W
    row = jnp.repeat(jnp.arange(rows), GRID_W).astype(jnp.float32)
    col = jnp.tile(jnp.arange(GRID_W), rows).astype(jnp.float32)
    inv = ROPE_THETA ** (-jnp.arange(0, AXIS_ROPE_DIM, 2, dtype=jnp.float32) / AXIS_ROPE_DIM)
    ang = jnp.concatenate([row[:, None] * inv, col[:, None] * inv], axis=-1)
    return jnp.cos(ang), jnp.sin(ang)

def apply_rope(t, cos, sin):
    t1, t2 = t[..., 0::2], t[..., 1::2]
    c = cos[None, :, None, :].astype(t.dtype)
    s = sin[None, :, None, :].astype(t.dtype)
    return jnp.stack([t1 * c - t2 * s, t1 * s + t2 * c], axis=-1).reshape(t.shape)

def features(h, w_in, qn, kn, rope):
    B_, L, _ = h.shape
    split_at = np.cumsum(PROJ_SIZES)[:-1].tolist()
    aq, ak, av, bq, bk, bv, cq, cf, cb, ci, cg, gates = jnp.split(h @ w_in, split_at, axis=-1)
    heads = lambda t, n: t.reshape(B_, L, n, HEAD_DIM)
    aq, ak, av = heads(aq, A_HEADS), heads(ak, A_KV_HEADS), heads(av, A_KV_HEADS)
    bq = rms_norm(heads(bq, B_HEADS), qn)
    bk = rms_norm(heads(bk, B_KV_HEADS), kn)
    bv = heads(bv, B_KV_HEADS)
    if rope is not None:
        cos, sin = rope
        aq, ak, bq, bk = [apply_rope(t, cos, sin) for t in (aq, ak, bq, bk)]
    return aq, ak, av, bq, bk, bv, cq, cf, cb, ci, cg, gates

def dense_attn(q, k, v, sink=None):
    B_, Lq, HQ, hd = q.shape
    KV = k.shape[2]
    G = HQ // KV
    s = jnp.einsum('bqkgd,bjkd->bkgqj', q.reshape(B_, Lq, KV, G, hd), k).astype(jnp.float32) * hd ** -0.5
    if sink is not None:
        s_sink = jnp.broadcast_to(sink.astype(jnp.float32).reshape(1, KV, G, 1, 1), s.shape[:-1] + (1,))
        s = jnp.concatenate([s, s_sink], axis=-1)
    p = jax.nn.softmax(s, axis=-1)[..., :k.shape[1]].astype(v.dtype)
    return jnp.einsum('bkgqj,bjkd->bqkgd', p, v).reshape(B_, Lq, HQ * hd)

def window_attn(q, k, v, ck, cv, sink):
    B_, S, HQ, hd = q.shape
    KV = k.shape[2]
    G = HQ // KV
    nb = S // BLOCK
    n_ctx = ck.shape[1]
    qb = q.reshape(B_, nb, BLOCK, KV, G, hd)

    def band(t):
        tp = jnp.pad(t, ((0, 0), (BLOCK, BLOCK), (0, 0), (0, 0))).reshape(B_, nb + 2, BLOCK, KV, hd)
        return jnp.concatenate([tp[:, :-2], tp[:, 1:-1], tp[:, 2:]], axis=2)

    kb, vb = band(k), band(v)
    scale = hd ** -0.5
    s_loc = jnp.einsum('bnqkgd,bnjkd->bkgnqj', qb, kb).astype(jnp.float32) * scale
    blk = jnp.arange(nb)[:, None, None]
    qpos = blk * BLOCK + jnp.arange(BLOCK)[None, :, None]
    kpos = (blk - 1) * BLOCK + jnp.arange(3 * BLOCK)[None, None, :]
    valid = (jnp.abs(kpos - qpos) <= WINDOW) & (kpos >= 0) & (kpos < S)
    s_loc = jnp.where(valid, s_loc, NEG_BIG)
    s_ctx = jnp.einsum('bnqkgd,bjkd->bkgnqj', qb, ck).astype(jnp.float32) * scale
    s_sink = jnp.broadcast_to(sink.astype(jnp.float32).reshape(1, KV, G, 1, 1, 1), s_ctx.shape[:-1] + (1,))
    p = jax.nn.softmax(jnp.concatenate([s_ctx, s_loc, s_sink], axis=-1), axis=-1).astype(v.dtype)
    o = (jnp.einsum('bkgnqj,bjkd->bnqkgd', p[..., :n_ctx], cv)
         + jnp.einsum('bkgnqj,bnjkd->bnqkgd', p[..., n_ctx:n_ctx + 3 * BLOCK], vb))
    return o.reshape(B_, S, HQ * hd)

def global_attn(q, k, v, ck, cv):
    B_, S, HQ, hd = q.shape
    nb = S // BLOCK
    k_all = jnp.concatenate([ck, k], axis=1)
    v_all = jnp.concatenate([cv, v], axis=1)
    qb = jnp.moveaxis(q.reshape(B_, nb, BLOCK, HQ, hd), 1, 0)
    o = lax.map(lambda qblk: dense_attn(qblk, k_all, v_all), qb)
    return jnp.moveaxis(o, 0, 1).reshape(B_, S, HQ * hd)

def layer_lower_bounds(raw):
    p = jax.nn.softmax(raw.astype(jnp.float32), axis=0)
    return jnp.clip(jnp.cumsum(p, axis=0) - p[0], 0.0, 1.0)

def hgrn_forget(z, lb):
    log_f = jax.nn.log_sigmoid(z) + jnp.log1p(lb * jnp.exp(-z))
    k = (1.0 - lb) * jax.nn.sigmoid(-z)
    return k, log_f

def gla_chunk_scan(q, k, v, log_f, s0):
    B_, L, H, _ = q.shape
    nc = L // CHUNK
    to_chunks = lambda t: t.reshape(B_, nc, CHUNK, H, t.shape[-1]).transpose(1, 0, 3, 2, 4)
    tri = jnp.tril(jnp.ones((CHUNK, CHUNK), dtype=bool))[:, :, None]

    def step(s, inp):
        qi, ki, vi, fi = inp
        a = jnp.cumsum(fi, axis=2)
        o_inter = jnp.einsum('bhtd,bhde->bhte', qi * jnp.exp(a), s)
        diff = a[:, :, :, None, :] - a[:, :, None, :, :]
        decay = jnp.exp(jnp.where(tri, diff, NEG_BIG))
        scores = jnp.einsum('bhtd,bhjd,bhtjd->bhtj', qi, ki, decay)
        o_intra = jnp.einsum('bhtj,bhje->bhte', scores, vi)
        a_last = a[:, :, -1, :]
        s_new = (jnp.exp(a_last)[..., None] * s
                 + jnp.einsum('bhjd,bhje->bhde', ki * jnp.exp(a_last[:, :, None, :] - a), vi))
        return s_new, o_inter + o_intra

    s_fin, o = lax.scan(step, s0, (to_chunks(q), to_chunks(k), to_chunks(v), to_chunks(log_f)))
    return o.transpose(1, 0, 3, 2, 4).reshape(B_, L, H, v.shape[-1]), s_fin

def hgrn2_bidir(cq, cf, cb, ci, cg, lb_f, lb_b, gn, s0_f, s0_b):
    B_, L = cq.shape[:2]
    q = jax.nn.silu(cq.astype(jnp.float32)).reshape(B_, L, C_HEADS, C_DK)
    v = ci.astype(jnp.float32).reshape(B_, L, C_HEADS, C_DV)
    k_f, lf_f = hgrn_forget(cf.astype(jnp.float32).reshape(B_, L, C_HEADS, C_DK), lb_f.reshape(C_HEADS, C_DK))
    k_b, lf_b = hgrn_forget(cb.astype(jnp.float32).reshape(B_, L, C_HEADS, C_DK), lb_b.reshape(C_HEADS, C_DK))
    rev = lambda t: jnp.flip(t, axis=1)
    o_f, s_f = gla_chunk_scan(q, k_f, v, lf_f, s0_f)
    o_b, s_b = gla_chunk_scan(rev(q), rev(k_b), rev(v), rev(lf_b), s0_b)
    o = rms_norm(o_f + rev(o_b), gn) * jax.nn.silu(cg.astype(jnp.float32)).reshape(B_, L, C_HEADS, C_DV)
    return o.reshape(B_, L, C_HEADS * C_DV).astype(cq.dtype), s_f, s_b

def merge_branches(ya, yb, yc, gates, w_branch, w_out):
    B_, L = ya.shape[:2]
    ys = jnp.stack([ya, yb, yc], axis=2)
    up = jnp.einsum('blnw,nwd->blnd', ys, w_branch)
    g = jax.nn.sigmoid(gates.reshape(B_, L, N_BRANCH, -1))
    return jnp.sum(g * up, axis=2) @ w_out

def dwconv(u, w, b):
    y = lax.conv_general_dilated(u, w[:, None, :], window_strides=(1,),
                                 padding=((CONV_W // 2, CONV_W // 2),),
                                 dimension_numbers=('NWC', 'WIO', 'NWC'),
                                 feature_group_count=u.shape[-1])
    return y + b

def conv_ffn(h, w_up, w_dw, b_dw, w_down):
    a, g = jnp.split(dwconv(h @ w_up, w_dw, b_dw), 2, axis=-1)
    return (a * jax.nn.silu(g)) @ w_down

def second_inputs(seed: int = 0) -> dict:
    key = jax.random.key(seed)
    ks = jax.random.split(key, 22)
    nrm = lambda k, shape, s: jax.random.normal(k, shape, jnp.float32) * s
    L = DEPTH_2
    return {
        'x': nrm(ks[0], (BATCH, SEQ, D_MODEL), 1.0),
        'c': nrm(ks[1], (BATCH, D_MODEL), 1.0),
        'ctx': nrm(ks[2], (BATCH, CTX_LEN, D_MODEL), 1.0),
        'c_ctx': nrm(ks[3], (D_MODEL,), 1.0),
        'w_mod': nrm(ks[4], (L, D_MODEL, N_MOD * D_MODEL), 0.5 * D_MODEL ** -0.5),
        'b_mod': nrm(ks[5], (L, N_MOD * D_MODEL), 0.02),
        'norm_mix': 1.0 + nrm(ks[6], (L, D_MODEL), 0.05),
        'norm_ffn': 1.0 + nrm(ks[7], (L, D_MODEL), 0.05),
        'w_in': nrm(ks[8], (L, D_MODEL, PROJ_WIDTH), D_MODEL ** -0.5),
        'sink_a': nrm(ks[9], (L, A_HEADS), 0.5),
        'qn_b': 1.0 + nrm(ks[10], (L, HEAD_DIM), 0.05),
        'kn_b': 1.0 + nrm(ks[11], (L, HEAD_DIM), 0.05),
        'lb_fwd': nrm(ks[12], (L, C_HEADS * C_DK), 1.0),
        'lb_bwd': nrm(ks[13], (L, C_HEADS * C_DK), 1.0),
        'gn_c': 1.0 + nrm(ks[14], (L, C_DV), 0.05),
        'w_branch': nrm(ks[15], (L, N_BRANCH, BRANCH_WIDTH, D_MODEL), BRANCH_WIDTH ** -0.5),
        'w_out': nrm(ks[16], (L, D_MODEL, D_MODEL), D_MODEL ** -0.5),
        'w_up': nrm(ks[17], (L, D_MODEL, 2 * D_FF), D_MODEL ** -0.5),
        'w_dw': nrm(ks[18], (L, CONV_W, 2 * D_FF), CONV_W ** -0.5),
        'b_dw': nrm(ks[19], (L, 2 * D_FF), 0.02),
        'w_down': nrm(ks[20], (L, D_FF, D_MODEL), D_FF ** -0.5),
        'norm_final': 1.0 + nrm(ks[21], (D_MODEL,), 0.05),
    }

def second_block(x, c, ctx, c_ctx, w_mod, b_mod, norm_mix, norm_ffn, w_in, sink_a, qn_b, kn_b,
              lb_fwd, lb_bwd, gn_c, w_branch, w_out, w_up, w_dw, b_dw, w_down, norm_final):
    B_, S, D = x.shape
    rope = axial_rope(S)
    lbf = layer_lower_bounds(lb_fwd)
    lbb = layer_lower_bounds(lb_bwd)
    s0 = jnp.zeros((B_, C_HEADS, C_DK, C_DV), jnp.float32)
    for l in range(DEPTH_2):
        last = l == DEPTH_2 - 1
        m_lat = (jax.nn.silu(c) @ w_mod[l] + b_mod[l]).reshape(B_, 1, N_MOD, D)
        m_ctx = (jax.nn.silu(c_ctx) @ w_mod[l] + b_mod[l]).reshape(N_MOD, D)

        h_lat = rms_norm(x, norm_mix[l]) * (1.0 + m_lat[:, :, 1]) + m_lat[:, :, 0]
        h_ctx = rms_norm(ctx, norm_mix[l]) * (1.0 + m_ctx[1]) + m_ctx[0]
        aq, ak, av, bq, bk, bv, cq, cf, cb, ci, cg, gates = features(h_lat, w_in[l], qn_b[l], kn_b[l], rope)
        caq, cak, cav, cbq, cbk, cbv, ccq, ccf, ccb, cci, ccg, cgates = features(h_ctx, w_in[l], qn_b[l], kn_b[l], None)

        yc_ctx, s_f, s_b = hgrn2_bidir(ccq, ccf, ccb, cci, ccg, lbf[l], lbb[l], gn_c[l], s0, s0)
        yc = hgrn2_bidir(cq, cf, cb, ci, cg, lbf[l], lbb[l], gn_c[l], s_f, s_b)[0]
        ya = window_attn(aq, ak, av, cak, cav, sink_a[l])
        yb = global_attn(bq, bk, bv, cbk, cbv)
        x_mix = x + m_lat[:, :, 2] * merge_branches(ya, yb, yc, gates, w_branch[l], w_out[l])

        h = rms_norm(x_mix, norm_ffn[l]) * (1.0 + m_lat[:, :, 4]) + m_lat[:, :, 3]
        x = x_mix + m_lat[:, :, 5] * conv_ffn(h, w_up[l], w_dw[l], b_dw[l], w_down[l])

        if not last:
            ya_c = dense_attn(caq, cak, cav, sink_a[l])
            yb_c = dense_attn(cbq, cbk, cbv)
            ctx_mix = ctx + m_ctx[2] * merge_branches(ya_c, yb_c, yc_ctx, cgates, w_branch[l], w_out[l])
            hc = rms_norm(ctx_mix, norm_ffn[l]) * (1.0 + m_ctx[4]) + m_ctx[3]
            ctx = ctx_mix + m_ctx[5] * conv_ffn(hc, w_up[l], w_dw[l], b_dw[l], w_down[l])
    return rms_norm(x, norm_final)


def setup_inputs(seed=0):
    out = dict(first_inputs(seed))
    for name, value in second_inputs(seed + 1).items():
        if name != "x":
            out[name + "_2"] = value
    return out


def reference(
    x, positions, meta_tokens, emb_ln_g, emb_ln_b, w_in, mla_q_norm, mla_kv_norm, mla_w_uq,
    mla_w_ukv, mla_out_norm, rwkv_mu_prev, rwkv_mu_next, rwkv_w0, rwkv_w2, rwkv_a0, rwkv_a2,
    rwkv_g2, rwkv_k_k, rwkv_k_a, rwkv_r_k, rwkv_gn_g, rwkv_gn_b, rwkv_v0, rwkv_v1, rwkv_v2,
    w_out, ln1_g, ln1_b, moe_w_group, moe_b_group, moe_w_expert, moe_b_expert, moe_w1, moe_w3,
    moe_w2, ln2_g, ln2_b, c_2, ctx_2, c_ctx_2, w_mod_2, b_mod_2, norm_mix_2, norm_ffn_2, w_in_2,
    sink_a_2, qn_b_2, kn_b_2, lb_fwd_2, lb_bwd_2, gn_c_2, w_branch_2, w_out_2, w_up_2, w_dw_2,
    b_dw_2, w_down_2, norm_final_2,
):
    x = first_block(
        x, positions, meta_tokens, emb_ln_g, emb_ln_b, w_in, mla_q_norm, mla_kv_norm, mla_w_uq,
        mla_w_ukv, mla_out_norm, rwkv_mu_prev, rwkv_mu_next, rwkv_w0, rwkv_w2, rwkv_a0, rwkv_a2,
        rwkv_g2, rwkv_k_k, rwkv_k_a, rwkv_r_k, rwkv_gn_g, rwkv_gn_b, rwkv_v0, rwkv_v1, rwkv_v2,
        w_out, ln1_g, ln1_b, moe_w_group, moe_b_group, moe_w_expert, moe_b_expert, moe_w1,
        moe_w3, moe_w2, ln2_g, ln2_b,
    )
    return second_block(
        x, c_2, ctx_2, c_ctx_2, w_mod_2, b_mod_2, norm_mix_2, norm_ffn_2, w_in_2, sink_a_2,
        qn_b_2, kn_b_2, lb_fwd_2, lb_bwd_2, gn_c_2, w_branch_2, w_out_2, w_up_2, w_dw_2, b_dw_2,
        w_down_2, norm_final_2,
    )


_drawn_inputs = setup_inputs


def setup_inputs(seed=0):
    import zlib

    import numpy as np

    out = dict(_drawn_inputs(seed))
    spreads = {}
    factors = {'mla_q_norm': 7.266,
     'mla_kv_norm': 4.391,
     'mla_out_norm': 6.364,
     'rwkv_w2': 3.988,
     'rwkv_k_k': 8.0,
     'rwkv_k_a': 4.52,
     'rwkv_gn_g': 8.0,
     'rwkv_gn_b': 8.0,
     'rwkv_v0': 2.859,
     'moe_b_group': 8.0,
     'moe_b_expert': 8.0,
     'ctx_2': 4.554,
     'b_mod_2': 2.849,
     'norm_mix_2': 7.13,
     'norm_ffn_2': 9.616,
     'sink_a_2': 8.0,
     'qn_b_2': 8.0,
     'kn_b_2': 8.0,
     'gn_c_2': 8.0,
     'b_dw_2': 22.762}
    for name, (base, spread) in spreads.items():
        noise = np.random.default_rng([zlib.crc32(name.encode()), seed]).standard_normal(out[name].shape)
        drawn = base * np.exp(spread * noise) if base else spread * noise
        out[name] = jnp.asarray(drawn.astype(out[name].dtype))
    for name, factor in factors.items():
        out[name] = (out[name] * factor).astype(out[name].dtype)
    return out
```

```python
from contextlib import ExitStack

import numpy as np

import concourse.bass as bass
from concourse import mybir

P = 128
D = 1024
KD = D // P
SEQ, META = 512, 16
T = SEQ + META
TC = 88
NC1 = T // TC
HT = T // 2
LAYERS = 2
H_A, NOPE, ROPE, VD = 4, 128, 64, 128
Q_LORA, KV_LORA = 256, 128
H_B, N_B = 8, 64
RW = H_B * N_B
RT = RW // P
MLA_COLS = Q_LORA + KV_LORA + ROPE
IN_COLS = MLA_COLS + 3 * RW + 384
UT = (IN_COLS - MLA_COLS) // P
GROUPS, PER_GROUP = 4, 8
EXPERTS = GROUPS * PER_GROUP
EH = 256
SLOT = 64
NBLK = (2 * T + EXPERTS * (SLOT - 1)) // SLOT
NBLK += NBLK % 2
ROWS = NBLK * SLOT
ALPHA = (2 * LAYERS) ** 0.25
LN_EPS, RMS_EPS, GN_EPS, KK_EPS = 1e-5, 1e-6, 64e-5, 1e-12
LEVELS1 = 7
PACK = 32
PACKED = 5
DECAY = float(np.exp(-0.5))

CTX = 256
LT, CT = SEQ // P, CTX // P
ST = LT + CT
NFF = 2816
FT = NFF // P
LEVELS2 = 7
NEG = -1e30

F32 = mybir.dt.float32
I32 = mybir.dt.int32
U32 = mybir.dt.uint32
ALU = mybir.AluOpType
ACT = mybir.ActivationFunctionType
AX = mybir.AxisListType

PARAMS1 = [("q_norm", 2), ("kv_norm", 1), ("out_norm", 4), ("mu_prev", UT), ("mu_next", UT),
           ("w0", 2 * RT), ("a0", 2 * RT), ("k_k", RT), ("k_a", RT), ("r_k", RT), ("gn_g", RT),
           ("gn_b", RT), ("ln1_g", KD), ("ln1_b", KD), ("ln2_g", KD), ("ln2_b", KD)]
COL1, _n = {}, 0
for _name, _w in PARAMS1:
    COL1[_name] = _n
    _n += _w
NPAR1 = _n
PARAMS2 = [("v0", RT), ("emb_g", KD), ("emb_b", KD), ("c", KD), ("c_ctx", KD), ("b_mod", 6 * KD),
           ("norm_mix", KD), ("norm_ffn", KD), ("qn", 1), ("kn", 1), ("gn_c", 1),
           ("w_dw", 3 * 2 * FT), ("b_dw", 2 * FT), ("norm_final", KD)]
COL2, _n = {}, 0
for _name, _w in PARAMS2:
    COL2[_name] = _n
    _n += _w
NPAR2 = _n
EPS_COLS = {"ln": 0, "rms": 1, "kk": 2, "gn": 3, "one": 4, "halfpi": 5}


class Chain:

    def __init__(self, eng, sem):
        self.eng, self.sem, self.n = eng, sem, 0

    def mark(self, ins):
        ins.then_inc(self.sem, 1)
        self.n += 1

    def __call__(self, ins):
        self.mark(ins)
        self.eng.wait_ge(self.sem, self.n)

    def sync(self):
        self.eng.wait_ge(self.sem, self.n)


class Kernel:

    def __init__(self, nc):
        self.nc = nc
        self.top = ExitStack()
        self.stages = 0
        self.pool_sems = {}

    def sb(self, name, shape, dt=F32, stack=None):
        return (stack or self.top).enter_context(self.nc.sbuf_tensor(name, shape, dt))

    def stage(self, *names):
        return Stage(self, names)

    def pool_dma_sems(self, *names):
        for n in names:
            self.pool_sems[n] = self.top.enter_context(self.nc.semaphore(n))


class Stage:

    def __init__(self, k, names):
        self.k, self.names = k, names

    def __enter__(self):
        k = self.k
        self.stack = ExitStack()
        self.i = k.stages
        k.stages += 1
        self.sems = [k.pool_sems[n] if n in k.pool_sems else
                     self.stack.enter_context(k.nc.semaphore(f"{n}_{self.i}")) for n in self.names]
        self.block = k.nc.Block()
        self.b = self.block.__enter__()
        return (self.b, *self.sems)

    def __exit__(self, *exc):
        self.block.__exit__(*exc)
        if exc[0] is None:
            with self.k.nc.Block() as clear:
                pool = [s for n, s in zip(self.names, self.sems) if n in self.k.pool_sems]
                sems = [s for n, s in zip(self.names, self.sems) if n not in self.k.pool_sems]

                @clear.sync
                def _(sp):
                    for s in sems:
                        sp.sem_clear(s)

                if pool:
                    @clear.gpsimd
                    def _(gp):
                        for s in pool:
                            gp.dma_reset(range(s.num, s.num + 1))
                            gp.sem_clear(s)
        self.stack.__exit__(*exc)


def split2(ap):
    return ap.rearrange("p (a b) -> p a b", a=2)


def linear(k, name, strips, evac, on="vector", before=()):
    nc, ps = k.nc, k.ps
    tiles = [(s, key, outs) for s, (_, ts) in enumerate(strips) for key, outs in ts]
    upto = np.cumsum([len(ts) for _, ts in strips]).tolist()
    loads = [len(ld) for ld, _ in strips]
    with k.stage(f"{name}_w_even", f"{name}_w_odd", f"{name}_product", f"{name}_emptied",
                 f"{name}_chain") as (block, w_even, w_odd, product, emptied, steps):
        landed = (w_even, w_odd)

        @block.sync
        def _(sp):
            for s, (ld, _) in enumerate(strips):
                if s >= 2 and ld:
                    sp.wait_ge(product, upto[s - 2])
                for dst, src in ld:
                    sp.dma_start(dst, src).then_inc(landed[s % 2], 16)

        @block.tensor
        def _(pe):
            got = [0, 0]
            last_s = -1
            for t, (s, key, outs) in enumerate(tiles):
                if s != last_s:
                    for z in range(last_s + 1, s + 1):
                        got[z % 2] += 16 * loads[z]
                    last_s = s
                    if loads[s]:
                        pe.wait_ge(landed[s % 2], got[s % 2])
                if t >= 4:
                    pe.wait_ge(emptied, t - 3)
                bank = 2 * (t % 4)
                for off, cols, rows, pairs in outs:
                    for n, (lhsT, rhs) in enumerate(pairs):
                        last = pe.matmul(ps[0:rows, bank + off, 0:cols], lhsT=lhsT, rhs=rhs,
                                         start=(n == 0), stop=(n == len(pairs) - 1))
                last.then_inc(product, 1)

        def empty(eng):
            chain = Chain(eng, steps)
            for t, (s, key, outs) in enumerate(tiles):
                if t:
                    eng.wait_ge(emptied, t)
                eng.wait_ge(product, t + 1)
                evac(eng, chain, key, 2 * (t % 4)).then_inc(emptied, 1)

        if on == "vector":
            block.vector(empty)
        else:
            block.scalar(empty)


def halves(pairs, rows=P):
    return [(h, HT, rows, [(l, r[..., h * HT:(h + 1) * HT]) for l, r in pairs]) for h in range(2)]


def inv_root(k, eng, chain, out, eps_free):
    chain(eng.reciprocal(out, eps_free))


def layer_norm(k, z, gain, bias, out, scratch, stat):
    nc, ps, cst = k.nc, k.ps, k.cst
    mean_w = k.ones_d
    with k.stage("ln_summed", "ln_centred", "ln_squared", "ln_root", "ln_scale", "ln_chain",
                 "ln_act") as (block, summed, centred, squared, root, scaled, steps, acts):
        @block.tensor
        def _(pe):
            for h in range(2):
                for i in range(KD):
                    last = pe.matmul(ps[:, h, 0:HT], lhsT=mean_w, rhs=z[:, i, h * HT:(h + 1) * HT],
                                     start=(i == 0), stop=(i == KD - 1))
            last.then_inc(summed, 1)
            for i in range(KD):
                pe.wait_ge(squared, i + 1)
                for h in range(2):
                    last = pe.matmul(ps[:, 2 + h, 0:HT], lhsT=mean_w,
                                     rhs=scratch[:, i, h * HT:(h + 1) * HT],
                                     start=(i == 0), stop=(i == KD - 1))
            last.then_inc(summed, 1)

        @block.vector
        def _(dve):
            chain = Chain(dve, steps)
            dve.wait_ge(summed, 1)
            chain(dve.tensor_copy(split2(stat), ps[:, 0:2, 0:HT]))
            for i in range(KD):
                dve.tensor_tensor(z[:, i, :], z[:, i, :], stat, ALU.subtract).then_inc(centred, 1)
            dve.wait_ge(root, 1)
            chain(dve.reciprocal(stat, stat))
            dve.wait_ge(centred, KD)
            for i in range(KD):
                dve.tensor_tensor(z[:, i, :], z[:, i, :], stat, ALU.mult).then_inc(scaled, 1)

        @block.scalar
        def _(act):
            for i in range(KD):
                act.wait_ge(centred, i + 1)
                act.activation(scratch[:, i, :], z[:, i, :], ACT.Square).then_inc(squared, 1)
            act.wait_ge(summed, 2)
            act.activation(split2(stat), ps[:, 2:4, 0:HT], ACT.Sqrt,
                           bias=k.eps("ln")).then_inc(root, 1)
            for i in range(KD):
                act.wait_ge(scaled, i + 1)
                act.activation(out[:, i, :], z[:, i, :], ACT.Identity, bias=bias[:, i:i + 1],
                               scale=gain[:, i:i + 1]).then_inc(acts, 1)


def embed(k, a):
    nc, ps = k.nc, k.ps
    with ExitStack() as tmp:
        rows = k.sb("rows", [TC, NC1, D], stack=tmp)
        sq = k.sb("emb_sq", [TC, D], stack=tmp)
        st = k.sb("emb_st", [TC, 4, NC1], stack=tmp)
        with k.stage("x_landed", "emb_stat", "emb_root", "emb_ready", "emb_turned", "emb_copied",
                     "emb_chain") as (block, landed, stat, root, ready, turned, copied, steps):
            @block.sync
            def _(sp):
                sp.dma_start(rows[0:META, 0, :], a["meta_tokens"]).then_inc(landed, 16)
                sp.dma_start(rows[META:TC, 0, :], a["x"][0, 0:TC - META, :]).then_inc(landed, 16)
                for j in range(1, NC1):
                    sp.dma_start(rows[:, j, :],
                                 a["x"][0, j * TC - META:(j + 1) * TC - META, :]).then_inc(landed, 16)

            @block.vector
            def _(dve):
                chain = Chain(dve, steps)
                dve.wait_ge(landed, 16 * (NC1 + 1))
                for j in range(NC1):
                    dve.tensor_reduce(st[:, 0, j:j + 1], rows[:, j, :], AX.X, ALU.add).then_inc(steps, 1)
                    chain.n += 1
                chain.sync()
                chain(dve.tensor_scalar(st[:, 1, :], st[:, 0, :], 1.0 / D, None, ALU.mult))
                for j in range(NC1):
                    chain(dve.tensor_scalar(rows[:, j, :], rows[:, j, :], st[:, 1, j:j + 1], None,
                                            ALU.subtract))
                    chain(dve.tensor_tensor(sq[:, :], rows[:, j, :], rows[:, j, :], ALU.mult))
                    chain(dve.tensor_reduce(st[:, 2, j:j + 1], sq[:, :], AX.X, ALU.add))
                dve.nop().then_inc(stat, 1)
                dve.wait_ge(root, 1)
                chain(dve.reciprocal(st[:, 3, :], st[:, 3, :]))
                for j in range(NC1):
                    dve.tensor_scalar(rows[:, j, :], rows[:, j, :], st[:, 3, j:j + 1], None,
                                      ALU.mult).then_inc(ready, 1)

            @block.scalar
            def _(act):
                act.wait_ge(stat, 1)
                act.activation(st[:, 3, :], st[:, 2, :], ACT.Sqrt, bias=k.eps("ln")[0:TC, :],
                               scale=1.0 / D).then_inc(root, 1)
                for u in range(NC1 * 2):
                    j, q = u // 2, u % 2
                    act.wait_ge(turned, u + 1)
                    for i in range(4):
                        f = 4 * q + i
                        last = act.activation(
                            k.h[:, f, j * TC:(j + 1) * TC], ps[:, u % 4, i * TC:(i + 1) * TC],
                            ACT.Identity, bias=k.p2("emb_b", f), scale=k.p2("emb_g", f))
                    last.then_inc(copied, 1)

            @block.tensor
            def _(pe):
                for u in range(NC1 * 2):
                    j, q = u // 2, u % 2
                    pe.wait_ge(ready, j + 1)
                    if u >= 4:
                        pe.wait_ge(copied, u - 3)
                    for i in range(4):
                        f = 4 * q + i
                        last = pe.transpose(ps[:, u % 4, i * TC:(i + 1) * TC],
                                            rows[:, j, f * P:(f + 1) * P], k.ident[0:TC, 0:TC])
                    last.then_inc(turned, 1)


def rotary_tables(k, a):
    nc = k.nc
    two_pi = 2 * np.pi
    c1 = 6.28125
    c2 = float(np.float32(np.floor((two_pi - c1) * 2 ** 20) / 2 ** 20))
    c3 = float(np.float32(two_pi - c1 - c2))
    magic = 1.5 * 2 ** 23
    with ExitStack() as tmp:
        pos = k.sb("pos", [P, T], I32, stack=tmp)
        ang = k.sb("ang", [P, T], stack=tmp)
        turn = k.sb("turn", [P, T], stack=tmp)
        w = k.sb("wrap", [P, T], stack=tmp)
        with k.stage("pos_landed", "ang_ready", "trig_chain") as (block, landed, ready, steps):
            @block.sync
            def _(sp):
                sp.dma_start(pos[:, META:T], a["positions"].to_broadcast([P, SEQ])).then_inc(landed, 16)

            @block.gpsimd
            def _(gp):
                gp.iota(pos[:, 0:META], pattern=[[1, META]], base=-META,
                        channel_multiplier=0).then_inc(landed, 16)

            @block.vector
            def _(dve):
                chain = Chain(dve, steps)
                dve.wait_ge(landed, 32)
                chain(dve.tensor_copy(ang[:, :], pos[:, :]))
                chain(dve.tensor_scalar(ang[:, :], ang[:, :], float(META), k.cst[:, 6:7], ALU.add, ALU.mult))
                chain(dve.tensor_scalar(turn[:, :], ang[:, :], 1 / two_pi, magic, ALU.mult, ALU.add))
                chain(dve.tensor_scalar(turn[:, :], turn[:, :], -magic, None, ALU.add))
                for c in (c1, c2, c3):
                    chain(dve.scalar_tensor_tensor(ang[:, :], turn[:, :], -c, ang[:, :], ALU.mult, ALU.add))
                chain(dve.tensor_scalar(turn[:, :], ang[:, :], float(np.pi / 2), None, ALU.add))
                chain(dve.tensor_scalar(w[:, :], turn[:, :], float(np.pi), -two_pi, ALU.is_gt, ALU.mult))
                chain(dve.tensor_tensor(turn[:, :], turn[:, :], w[:, :], ALU.add))
                for t in (ang, turn):
                    chain(dve.tensor_scalar(t[:, :], t[:, :], 3.1415925, -3.1415925, ALU.min, ALU.max))
                dve.nop().then_inc(ready, 1)

            @block.scalar
            def _(act):
                act.wait_ge(ready, 1)
                act.activation(k.sin[:, :], ang[:, :], ACT.Sin)
                act.activation(k.cos[:, :], turn[:, :], ACT.Sin)


def load_layer_params(k, a, li):
    nc = k.nc
    uq = a["mla_w_uq"][bass.ds(li, 1), :, :].rearrange("a (t p) (h c) -> (a t) p h c", p=P, h=H_A)
    with k.stage("params_landed") as (block, landed):
        @block.sync
        def _(sp):
            loads = [(k.par1[:, :], a["par1"][bass.ds(li, 1), :, :].rearrange("a p n -> (a p) n")),
                     *[(k.w_uq[:, t, 0:H_A * NOPE].rearrange("p (h c) -> p h c", h=H_A), uq[t, :, :, 0:NOPE])
                       for t in range(2)],
                     *[(k.w_uq[:, t, H_A * NOPE:].rearrange("p (h c) -> p h c", h=H_A), uq[t, :, :, NOPE:])
                       for t in range(2)],
                     (k.w_ukv[:, :], a["mla_w_ukv"][bass.ds(li, 1), :, :].rearrange("a p n -> (a p) n")),
                     (k.w2[:, :], a["rwkv_w2"][bass.ds(li, 1), :, :, :].rearrange("a d r n -> (a d r) n")),
                     (k.a2[:, :], a["rwkv_a2"][bass.ds(li, 1), :, :, :].rearrange("a d r n -> (a d r) n")),
                     (k.g2[:, :], a["rwkv_g2"][bass.ds(li, 1), :, :].rearrange("a p n -> (a p) n"))]
            for dst, src in loads:
                sp.dma_start(dst, src).then_inc(landed, 16)
            sp.wait_ge(landed, 16 * len(loads))


def project_in(k, a, li, ring, pad):
    w = a["w_in"][bass.ds(li, 1), :, :].rearrange("a (t p) n -> p (a t) n", p=P)
    strips = []
    buf = ring[0]
    loads = [(buf[:, :, 0:MLA_COLS], w[:, :, 0:MLA_COLS]),
             (buf[:, :, MLA_COLS:MLA_COLS + ROPE], w[:, :, MLA_COLS - ROPE:MLA_COLS])]
    strips.append((loads, [(("mla", m), halves([(buf[:, i, m * P:(m + 1) * P], k.h[:, i, :])
                                                for i in range(KD)])) for m in range(4)]))
    per = 3
    for s in range(UT // per):
        buf = ring[(s + 1) % 2]
        c0 = MLA_COLS + s * per * P
        strips.append(([(buf[:, :, 0:per * P], w[:, :, c0:c0 + per * P])],
                       [(("u", s * per + m), halves([(buf[:, i, m * P:(m + 1) * P], k.h[:, i, :])
                                                     for i in range(KD)])) for m in range(per)]))

    def evac(dve, chain, key, bank):
        kind, m = key
        if kind == "mla":
            return dve.tensor_copy(split2(k.mla[:, m, :]), k.ps[:, bank:bank + 2, 0:HT])
        u = k.u[:, m, :]
        chain(dve.tensor_copy(pad[:, 1:T + 1].rearrange("p (a b) -> p a b", a=2),
                              k.ps[:, bank:bank + 2, 0:HT]))
        chain(dve.tensor_scalar(u, pad[:, 1:T + 1], k.keep[:, m:m + 1], None, ALU.mult))
        chain(dve.scalar_tensor_tensor(u, pad[:, 0:T], k.p1("mu_prev", m), u, ALU.mult, ALU.add))
        return dve.scalar_tensor_tensor(u, pad[:, 2:T + 2], k.p1("mu_next", m), u, ALU.mult, ALU.add)

    with k.stage("pad_chain") as (block, steps):
        @block.vector
        def _(dve):
            chain = Chain(dve, steps)
            chain(dve.memset(pad[:, :], 0.0))
            c0, c1 = COL1["mu_prev"], COL1["mu_next"]
            chain(dve.tensor_tensor(k.keep[:, :], k.par1[:, c0:c0 + UT], k.par1[:, c1:c1 + UT], ALU.add))
            chain(dve.tensor_scalar(k.keep[:, :], k.keep[:, :], -1.0, 1.0, ALU.mult, ALU.add))
    linear(k, "w_in", strips, evac)


def rms_scale(k, name, parts, width, ones, eps, scratch, stat):
    nc, ps = k.nc, k.ps
    flat = [(n, i, t) for n, ts in enumerate(parts) for i, t in enumerate(ts)]
    cols = parts[0][0].shape[-1]
    half = cols // 2
    with k.stage(f"{name}_squared", f"{name}_summed", f"{name}_root", f"{name}_chain") as (
            block, squared, summed, root, steps):
        @block.vector
        def _(dve):
            for q, (n, i, t) in enumerate(flat):
                dve.tensor_tensor(scratch[:, q, 0:cols], t, t, ALU.mult).then_inc(squared, 1)
            for n in range(len(parts)):
                dve.wait_ge(root, n + 1)
                dve.reciprocal(stat[:, n, 0:cols], stat[:, n, 0:cols]).then_inc(steps, 1)

        @block.tensor
        def _(pe):
            q = 0
            for n, ts in enumerate(parts):
                pe.wait_ge(squared, q + len(ts))
                if n >= 4:
                    pe.wait_ge(root, n - 3)
                for h in range(2):
                    for i in range(len(ts)):
                        last = pe.matmul(ps[:, 2 * (n % 4) + h, 0:half], lhsT=ones,
                                         rhs=scratch[:, q + i, h * half:(h + 1) * half],
                                         start=(i == 0), stop=(i == len(ts) - 1))
                last.then_inc(summed, 1)
                q += len(ts)

        @block.scalar
        def _(act):
            for n in range(len(parts)):
                act.wait_ge(summed, n + 1)
                act.activation(split2(stat[:, n, 0:cols]),
                               ps[:, 2 * (n % 4):2 * (n % 4) + 2, 0:half], ACT.Sqrt,
                               bias=k.eps(eps), scale=1.0 / width).then_inc(root, 1)


def attention(k, name, units, groups, rows, pw, pt, small, masked=None):
    nc, ps = k.nc, k.ps
    n_u = len(units)
    last_of = {u["group"]: i for i, u in enumerate(units)}
    with k.stage(f"{name}_scored", f"{name}_peaked", f"{name}_weighed", f"{name}_normed",
                 f"{name}_turned", f"{name}_kept", f"{name}_summed", f"{name}_stored",
                 f"{name}_chain", f"{name}_extra") as (
            block, scored, peaked, weighed, normed, turned, kept, summed, stored, steps, extra):

        @block.tensor
        def _(pe):
            def score(i):
                if i >= 2:
                    pe.wait_ge(weighed, i - 1)
                for bank, cols, off, pairs in units[i]["score"]:
                    for n, (lhsT, rhs) in enumerate(pairs):
                        last = pe.matmul(ps[0:rows, 2 * (i % 2) + bank, off:off + cols],
                                         lhsT=lhsT, rhs=rhs, start=(n == 0),
                                         stop=(n == len(pairs) - 1))
                last.then_inc(scored, 1)

            for i in range(min(2, n_u)):
                score(i)
            for v, u in enumerate(units):
                if v + 2 < n_u:
                    score(v + 2)
                g = u["group"]
                pe.wait_ge(normed, v + 1)
                if v >= 1:
                    pe.wait_ge(kept, v)
                for n, (off, w) in enumerate(u["tiles"]):
                    last = pe.transpose(ps[0:w, 4 + n // 3, (n % 3) * rows:(n % 3 + 1) * rows],
                                        pw[0:rows, v % 2, off:off + w], k.ident[0:rows, 0:rows])
                last.then_inc(turned, 1)
                if last_of[g] == v:
                    pe.wait_ge(kept, v + 1)
                    if g >= 1:
                        pe.wait_ge(stored, g)
                    grp = groups[g]
                    for bank, orows, q0, qn in grp["outs"]:
                        for n, (val, (_, w)) in enumerate(zip(grp["values"], u["tiles"])):
                            last = pe.matmul(ps[0:orows, 6 + bank, 0:qn], lhsT=val,
                                             rhs=pt[0:w, g % 2, n, q0:q0 + qn], start=(n == 0),
                                             stop=(n == len(grp["values"]) - 1))
                    last.then_inc(summed, 1)

        @block.vector
        def _(dve):
            chain = Chain(dve, steps)
            for i in range(n_u + 1):
                if i < n_u:
                    u = units[i]
                    dve.wait_ge(scored, i + 1)
                    if masked:
                        if i >= 2:
                            dve.wait_ge(weighed, i - 1)
                        masked(dve, chain, u, i)
                    m = small[0:rows, i % 2, 0:1]
                    if masked:
                        chain(dve.tensor_reduce(m, u["span"], AX.X, ALU.max))
                        chain(dve.tensor_scalar(m, m, u["sink"], -1.0, ALU.max, ALU.mult))
                    else:
                        chain(dve.tensor_reduce(m, u["span"], AX.XY, ALU.max))
                        chain(dve.tensor_scalar(m, m, -u["scale"], None, ALU.mult))
                    dve.nop().then_inc(peaked, 1)
                if i >= 1:
                    v = i - 1
                    u = units[v]
                    dve.wait_ge(weighed, v + 1)
                    s = small[0:rows, v % 2, 1:2]
                    if masked:
                        chain(dve.tensor_tensor(s, s, small[0:rows, v % 2, 2:3], ALU.add))
                    chain(dve.reciprocal(s, s))
                    p = pw[0:rows, v % 2, 0:u["keys"]]
                    dve.tensor_scalar(p, p, s, None, ALU.mult).then_inc(normed, 1)
                    dve.wait_ge(normed, v + 1)
                    g = u["group"]
                    if g >= 1 and (v == 0 or units[v - 1]["group"] != g):
                        dve.wait_ge(summed, g)
                        groups[g - 1]["store"](dve, chain).then_inc(stored, 1)
            dve.wait_ge(summed, len(groups))
            groups[-1]["store"](dve, chain).then_inc(stored, 1)

        @block.scalar
        def _(act):
            for i in range(n_u + 1):
                if i < n_u:
                    u = units[i]
                    act.wait_ge(peaked, i + 1)
                    if i >= 2:
                        act.wait_ge(turned, i - 1)
                    act.activation(u["dst"], u["span"], ACT.Exp, bias=small[0:rows, i % 2, 0:1],
                                   scale=1.0 if masked else u["scale"],
                                   accum_out=small[0:rows, i % 2, 1:2]).then_inc(
                                       extra if masked else weighed, 1)
                    if masked:
                        act.activation(small[0:rows, i % 2, 2:3], u["sink"], ACT.Exp,
                                       bias=small[0:rows, i % 2, 0:1]).then_inc(weighed, 1)
                if i >= 1:
                    v = i - 1
                    u = units[v]
                    g = u["group"]
                    act.wait_ge(turned, v + 1)
                    if g >= 2 and (v == 0 or units[v - 1]["group"] != g):
                        act.wait_ge(summed, g - 1)
                    nt = len(u["tiles"])
                    q0 = u["at"]
                    for b in range(0, nt, 3):
                        m = min(3, nt - b)
                        w = u["tiles"][b][1]
                        src = ps[0:w, 4 + b // 3, 0:m * rows].rearrange("p (n q) -> p n q", n=m)
                        last = act.activation(pt[0:w, g % 2, b:b + m, q0:q0 + rows], src, ACT.Copy)
                        if b + 3 < nt:
                            last.then_inc(extra, 1)
                    last.then_inc(kept, 1)


def rope(k, name, tiles, rot, cos, sin, tmp):
    nc, ps = k.nc, k.ps
    cols = tiles[0].shape[-1]
    half = cols // 2
    with k.stage(f"{name}_partner", f"{name}_done", f"{name}_chain") as (block, partner, done, steps):
        @block.tensor
        def _(pe):
            for n, t in enumerate(tiles):
                if n >= 4:
                    pe.wait_ge(done, n - 3)
                for h in range(2):
                    last = pe.matmul(ps[:, 2 * (n % 4) + h, 0:half], lhsT=rot,
                                     rhs=t[:, h * half:(h + 1) * half], start=True, stop=True)
                last.then_inc(partner, 1)

        @block.vector
        def _(dve):
            chain = Chain(dve, steps)
            for n, t in enumerate(tiles):
                dve.wait_ge(partner, n + 1)
                chain(dve.tensor_tensor(split2(tmp[:, 0:cols]),
                                        ps[:, 2 * (n % 4):2 * (n % 4) + 2, 0:half], split2(sin),
                                        ALU.mult))
                chain(dve.tensor_tensor(t, t, cos, ALU.mult))
                dve.tensor_tensor(t, t, tmp[:, 0:cols], ALU.add).then_inc(done, 1)
                dve.wait_ge(done, n + 1)


def mla(k, a):
    nc, ps = k.nc, k.ps
    scale = float(NOPE + ROPE) ** -0.5
    with ExitStack() as tmp:
        sq = k.sb("mla_sq", [P, 4, T], stack=tmp)
        st = k.sb("mla_st", [P, 2, T], stack=tmp)
        q = k.sb("mla_q", [P, 6, T], stack=tmp)
        kn = k.sb("mla_k", [P, H_A, T], stack=tmp)
        v = k.sb("mla_v", [TC, NC1, H_A * VD], stack=tmp)
        rms_scale(k, "c_q", [[k.mla[:, 0, :], k.mla[:, 1, :]]], Q_LORA, k.ones[:, :], "rms", sq,
                  st[:, 0:1, :])
        rms_scale(k, "c_kv", [[k.mla[:, 2, :]]], KV_LORA, k.ones[:, :], "rms", sq, st[:, 1:2, :])
        with k.stage("c_chain") as (block, steps):
            @block.vector
            def _(dve):
                for i in range(3):
                    gain = k.p1("q_norm", i) if i < 2 else k.p1("kv_norm")
                    dve.scalar_tensor_tensor(k.mla[:, i, :], k.mla[:, i, :], gain,
                                             st[:, i // 2, :], ALU.mult, ALU.mult).then_inc(steps, 1)
        wk = k.w_ukv[:, :].rearrange("p (h c) -> p h c", h=H_A)
        tiles = []
        for m in range(6):
            def cols(i, m=m):
                return k.w_uq[:, i, m * P:(m + 1) * P]
            tiles.append((("q", m), halves([(cols(i), k.mla[:, i, :]) for i in range(2)])))
        for m in range(H_A):
            tiles.append((("k", m), halves([(wk[:, m, 0:NOPE], k.mla[:, 2, :])])))
        for j in range(NC1):
            tiles.append((("v", j), [(0, H_A * VD, TC, [(k.mla[:, 2, j * TC:(j + 1) * TC],
                                                          wk[:, :, NOPE:NOPE + VD])])]))

        def evac(dve, chain, key, bank):
            kind, m = key
            if kind == "v":
                return dve.tensor_copy(v[:, m, :], ps[0:TC, bank, :])
            return dve.tensor_copy(split2((q if kind == "q" else kn)[:, m, :]),
                                   ps[:, bank:bank + 2, 0:HT])
        linear(k, "qkv", [([], tiles)], evac)
        rope(k, "mla_rope", [q[:, 4, :], q[:, 5, :], k.mla[:, 3, :]], k.rot1[:, :], k.cos[:, :],
             k.sin[:, :], sq[:, 0, :])
        with ExitStack() as at:
            pw = k.sb("mla_p", [TC, 2, T], stack=at)
            pt = k.sb("mla_pt", [TC, 2, NC1, T], stack=at)
            small = k.sb("mla_small", [TC, 2, 4], stack=at)
            units, groups = [], []
            for h in range(H_A):
                b = ROPE * (h % 2)
                for j in range(NC1):
                    tok = slice(j * TC, (j + 1) * TC)
                    score = []
                    for half in range(2):
                        ks = slice(half * HT, (half + 1) * HT)
                        score.append((half, HT, 0, [
                            (q[:, h, tok], kn[:, h, ks]),
                            (q[b:b + ROPE, 4 + h // 2, tok], k.mla[b:b + ROPE, 3, ks])]))
                    i = len(units)
                    units.append(dict(group=h, score=score, keys=T, scale=scale, at=j * TC,
                                      span=ps[0:TC, 2 * (i % 2):2 * (i % 2) + 2, 0:HT],
                                      dst=split2(pw[:, i % 2, :]),
                                      tiles=[(n * TC, TC) for n in range(NC1)]))

                def store(dve, chain, h=h):
                    return dve.tensor_copy(split2(k.att[:, h, :]), ps[:, 6:8, 0:HT])
                groups.append(dict(values=[v[:, n, h * VD:(h + 1) * VD] for n in range(NC1)],
                                   outs=[(0, VD, 0, HT), (1, VD, HT, HT)], store=store))
            attention(k, "mla_att", units, groups, TC, pw[:, :, :], pt[:, :, :, :], small[:, :, :])
        rms_scale(k, "mla_out", [[k.att[:, h, :]] for h in range(H_A)], VD, k.ones[:, :], "rms", sq, q)
        with k.stage("att_chain") as (block, steps):
            @block.vector
            def _(dve):
                for h in range(H_A):
                    dve.scalar_tensor_tensor(k.att[:, h, :], k.att[:, h, :], k.p1("out_norm", h),
                                             q[:, h, :], ALU.mult, ALU.mult).then_inc(steps, 1)


def rwkv(k, a, li):
    nc, ps = k.nc, k.ps
    r, key, v = (k.u[:, n * RT:(n + 1) * RT, :] for n in range(3))
    decay_in, rate_in, gate_in = (k.u[:, 3 * RT + n, :] for n in range(3))
    with ExitStack() as tmp:
        kk = k.sb("kk", [P, RT, T], stack=tmp)
        sig = [k.sb(f"sig{d}", [P, RT, T], stack=tmp) for d in range(2)]
        rate = [k.sb(f"rate{d}", [P, RT, T], stack=tmp) for d in range(2)]
        y = k.sb("y", [P, RT, T], stack=tmp)
        with ExitStack() as pre:
            v1 = k.sb("v1", [P, RT, 32], stack=pre)
            v2 = k.sb("v2", [32, RW], stack=pre)
            low = k.sb("v_low", [32, T], stack=pre)
            vf = k.sb("v_first", [P, RT, T], stack=pre)
            with k.stage("v_out", "v_in", "lora_act", "kk_chain") as (block, v_out, v_in, acts, steps):
                @block.sync
                def _(sp):
                    sp.dma_start(k.v_dram[bass.ds(li, 1), :, :, :].rearrange("a p t n -> (a p) t n"),
                                 v).then_inc(v_out, 16)
                    sp.wait_ge(v_out, 16)
                    sp.dma_start(vf[:, :, :], k.v_dram[0, :, :, :]).then_inc(v_in, 16)
                    sp.dma_start(v1[:, :, :], a["rwkv_v1"][0].rearrange("(t p) n -> p t n", p=P)
                                 ).then_inc(v_in, 16)
                    sp.dma_start(v2[:, :], a["rwkv_v2"][0]).then_inc(v_in, 16)
                    sp.wait_ge(v_in, 48)

                @block.scalar
                def _(act):
                    act.activation(decay_in, decay_in, ACT.Tanh).then_inc(acts, 1)
                    act.activation(gate_in, gate_in, ACT.Sigmoid).then_inc(acts, 1)

                @block.vector
                def _(dve):
                    for i in range(RT):
                        dve.tensor_scalar(kk[:, i, :], key[:, i, :], k.p1("k_k", i), None,
                                          ALU.mult).then_inc(steps, 1)
                    dve.memset(y[:, :, :], 0.0).then_inc(steps, 1)
            linear(k, "v_down", [([], [("v", halves([(v1[:, i, :], v[:, i, :]) for i in range(RT)], 32))])],
                   lambda act, ch, key_, bank: act.activation(split2(low[:, :]), ps[0:32, bank:bank + 2, 0:HT],
                                                              ACT.Copy), on="scalar")
            tiles = [(("s", m), halves([(v2[:, m * P:(m + 1) * P], low[:, :])])) for m in range(RT)]
            for d in range(2):
                b = 64 * d
                for m in range(RT):
                    c = slice(m * P, (m + 1) * P)
                    tiles.append((("w0", d, m), halves([(k.w2[b:b + 64, c], decay_in[b:b + 64, :])])))
                    tiles.append((("a0", d, m), halves([(k.a2[b:b + 64, c], rate_in[b:b + 64, :])])))

            def evac(act, chain, key_, bank):
                if key_[0] == "s":
                    dst, bias = y[:, key_[1], :], k.p2("v0", key_[1])
                else:
                    name, d, m = key_
                    dst, bias = (sig if name == "w0" else rate)[d][:, m, :], k.p1(name, d * RT + m)
                return act.activation(split2(dst), ps[:, bank:bank + 2, 0:HT], ACT.Sigmoid, bias=bias)
            linear(k, "lora", [([], tiles)], evac, on="scalar")
            with k.stage("v_chain") as (block, steps):
                @block.vector
                def _(dve):
                    chain = Chain(dve, steps)
                    chain(dve.tensor_tensor(vf[:, :, :], vf[:, :, :], v, ALU.subtract))
                    chain(dve.tensor_tensor(vf[:, :, :], vf[:, :, :], y[:, :, :], ALU.mult))
                    chain(dve.tensor_tensor(v, v, vf[:, :, :], ALU.add))
                    chain(dve.memset(y[:, :, :], 0.0))
            sq = k.sb("kk_sq", [P, RT, T], stack=pre)
            rms_scale(k, "kk", [[kk[:, i, :]] for i in range(RT)], 1.0, k.ones_h, "kk", sq, vf)
            with k.stage("kk_chain") as (block, steps):
                @block.vector
                def _(dve):
                    dve.tensor_tensor(kk[:, :, :], kk[:, :, :], vf[:, :, :], ALU.mult).then_inc(steps, 1)
        wkv(k, a, r, key, v, kk, sig, rate, y)
        rwkv_out(k, r, key, v, rate, y, gate_in, kk, sig)
        mix_out(k, a, li, y)


def wkv(k, a, r, key, v, kk, sig, rate, y):
    nc, ps = k.nc, k.ps
    HPT = 2
    G = 4
    with ExitStack() as tmp:
        def sb(name, shape, dt=F32):
            return k.sb(name, shape, dt, stack=tmp)
        masks = [sb("m_low", [TC, LEVELS1, TC], I32), sb("m_up", [TC, LEVELS1, TC], I32)]
        packed_masks = [sb("m_low_packed", [TC, PACKED, PACK], I32), sb("m_up_packed", [TC, PACKED, PACK], I32)]
        diag = sb("diag", [TC, TC + PACK])
        tri = sb("tri", [TC, 6, TC])
        reset = sb("reset", [P, 2, RT * TC])
        one_less = sb("one_less", [P, RT])
        state = [sb(f"state{d}", [P, RT, N_B]) for d in range(2)]
        D2 = range(2)
        e_pos = [sb(f"e_pos{d}", [P, RT, TC]) for d in D2]
        work = [sb(f"work{d}", [P, 4, RT * TC]) for d in D2]
        part = lambda d, n: work[d][:, n, :].rearrange("p (t n) -> p t n", t=RT)
        s_c = [part(d, 0) for d in D2]
        cum = [part(d, 1) for d in D2]
        e_neg = [part(d, 2) for d in D2]
        e_pre = [part(d, 3) for d in D2]
        kaprho = [sb(f"kaprho{d}", [P, RT, 2, TC]) for d in D2]
        bet = [sb(f"bet{d}", [P, RT, TC]) for d in D2]
        kh = [sb(f"kh{d}", [P, RT, TC]) for d in D2]
        vs = [sb(f"vs{d}", [P, RT, TC]) for d in D2]
        tok = [[sb(f"tok{n}{d}", [TC, RW]) for n in range(3)] for d in D2]
        grams = [[sb(f"gram{n}{g}", [TC, G, TC]) for n in range(4)] for g in range(4)]
        inv_t = [sb(f"inv_t{g}", [TC, G, TC]) for g in range(4)]
        inv = [sb(f"inv{g}", [TC, G, TC]) for g in range(4)]
        inv_p = [sb(f"inv_p{g}", [TC, G, PACK]) for g in range(4)]
        quarter = lambda g, n: work[g // 2][0:TC, 2 * (g % 2) + n, :]
        nt = [quarter(g, 0).rearrange("p (i q) -> p i q", i=G) for g in range(4)]
        nt_p = [quarter(g, 0)[:, 0:G * PACK].rearrange("p (i q) -> p i q", i=G) for g in range(4)]
        n_diag = [quarter(g, 1).rearrange("p (i q) -> p i q", i=G) for g in range(4)]
        over = lambda d, n: work[d][0:TC, 2 * n:2 * n + 2, :].rearrange("p a b -> p (a b)")[:, 0:RW]
        rn = [over(d, 0) for d in D2]
        us = [over(d, 1) for d in D2]
        with k.stage("wkv_const", "wkv_zero") as (block, landed, zeroed):
            @block.sync
            def _(sp):
                for dst, src in ((masks[0], "k_low"), (masks[1], "k_up"), (tri, "k_tri"),
                                 (packed_masks[0], "k_low_packed"), (packed_masks[1], "k_up_packed")):
                    sp.dma_start(dst[:, :, :], a[src]).then_inc(landed, 16)
                sp.dma_start(diag[:, :], a["k_diag"]).then_inc(landed, 16)
                sp.dma_start(reset[:, :, :], a["k_reset"].rearrange("p d t n -> p d (t n)")
                             ).then_inc(landed, 16)
                sp.wait_ge(landed, 16 * 7)

            @block.vector
            def _(dve):
                for d in D2:
                    dve.memset(state[d][:, :, :], 0.0).then_inc(zeroed, 1)
                c0 = COL1["k_a"]
                dve.tensor_scalar(one_less[:, :], k.par1[:, c0:c0 + RT], -1.0, 1.0, ALU.mult,
                                  ALU.add).then_inc(zeroed, 1)

        with nc.Fori(0, NC1) as c:
            off = [c * TC, (NC1 - 1) * TC - c * TC]
            cut = lambda t, d: t[:, :, bass.ds(off[d], TC)]
            with k.stage("cumulated", "cum_less", "decays", "pre_decays", "staged", "pool_chain",
                         "prep_chain") as (block, cumulated, less, decays, pre, staged, pool, steps):
                @block.gpsimd
                def _(gp):
                    chain = Chain(gp, pool)
                    c0 = COL1["k_a"]
                    ka = k.par1[:, c0:c0 + RT, None].to_broadcast([P, RT, TC])
                    for d in D2:
                        chain(gp.tensor_tensor(kh[d][:, :, :], cut(rate[d], d), ka, ALU.mult))
                        chain(gp.tensor_tensor(kh[d][:, :, :], kh[d][:, :, :],
                                               one_less[:, :, None].to_broadcast([P, RT, TC]), ALU.add))
                        chain(gp.tensor_tensor(kh[d][:, :, :], kh[d][:, :, :], cut(key, d), ALU.mult))
                        gp.tensor_copy(vs[d][:, :, :], cut(v, d)).then_inc(staged, 1)

                @block.vector
                def _(dve):
                    chain = Chain(dve, steps)
                    for d in D2:
                        chain(dve.tensor_copy(s_c[d][:, :, :], cut(sig[d], d)))
                        flat = lambda t: t.rearrange("p t n -> p (t n)")
                        o, m, x = flat(cum[d][:, :, :]), reset[:, d, :], flat(s_c[d][:, :, :])
                        if d:
                            o, m, x = o[:, ::-1], m[:, ::-1], x[:, ::-1]
                        dve.tensor_tensor_scan(o, m, x, 0.0, ALU.mult, ALU.add).then_inc(cumulated, 1)
                        dve.wait_ge(cumulated, d + 1)
                        dve.tensor_tensor(s_c[d][:, :, :], cum[d][:, :, :], s_c[d][:, :, :],
                                          ALU.subtract).then_inc(less, 1)
                        chain(dve.tensor_tensor(bet[d][:, :, :], cut(kk, d), cut(rate[d], d), ALU.mult))
                    for d in D2:
                        dve.wait_ge(decays, 2 * d + 2)
                        dve.tensor_tensor(bet[d][:, :, :], bet[d][:, :, :], e_neg[d][:, :, :],
                                          ALU.mult).then_inc(steps, 1)
                        dve.tensor_tensor(kaprho[d][:, :, 1, :], cut(r, d), e_pos[d][:, :, :],
                                          ALU.mult).then_inc(steps, 1)
                        dve.wait_ge(staged, d + 1)
                        dve.wait_ge(pool, 3 * d + 3)
                        dve.tensor_tensor(kh[d][:, :, :], kh[d][:, :, :], e_neg[d][:, :, :],
                                          ALU.mult).then_inc(steps, 1)
                        dve.wait_ge(pre, d + 1)
                        dve.tensor_tensor(kaprho[d][:, :, 0, :], cut(kk, d), e_pre[d][:, :, :],
                                          ALU.mult).then_inc(steps, 1)

                @block.scalar
                def _(act):
                    for d in D2:
                        act.wait_ge(cumulated, d + 1)
                        act.activation(e_neg[d][:, :, :], cum[d][:, :, :], ACT.Exp,
                                       scale=DECAY).then_inc(decays, 1)
                        act.activation(e_pos[d][:, :, :], cum[d][:, :, :], ACT.Exp,
                                       scale=-DECAY).then_inc(decays, 1)
                        act.wait_ge(less, d + 1)
                        act.activation(e_pre[d][:, :, :], s_c[d][:, :, :], ACT.Exp,
                                       scale=-DECAY).then_inc(pre, 1)

            with k.stage("turned", "tok_kept", "crossed", "masked", "n_cut", "t_set") as (
                    block, turned, kept, crossed, masked, n_cut, t_set):
                @block.gpsimd
                def _(gp):
                    eye = k.ident[0:TC, None, 0:TC].to_broadcast([TC, G, TC])
                    eye_p = diag[:, None, TC:TC + PACK].to_broadcast([TC, G, PACK])
                    for g in range(4):
                        gp.tensor_copy(inv[g][:, :, :], eye).then_inc(t_set, 1)
                        gp.tensor_copy(inv_t[g][:, :, :], eye).then_inc(t_set, 1)
                        gp.tensor_copy(inv_p[g][:, :, :], eye_p).then_inc(t_set, 1)

                @block.tensor
                def _(pe):
                    for n in range(6):
                        src = (bet, kh, vs)[n % 3][n // 3]
                        for f in range(RT):
                            last = pe.transpose(ps[0:TC, n, f * P:(f + 1) * P], src[:, f, :], k.ident)
                        last.then_inc(turned, 1)
                    for g in range(4):
                        d, b0 = g // 2, 4 * (g % 2)
                        if g < 2:
                            pe.wait_ge(kept, (4, 6)[g])
                        else:
                            pe.wait_ge(masked, 4 * (g - 1))
                        for n, lhs in enumerate((bet[d], kh[d])):
                            for i in range(G):
                                h = G * (g % 2) + i
                                b = N_B * (h % HPT)
                                last = pe.matmul(
                                    ps[0:TC, b0 + 2 * n + i % 2, (i // 2) * 2 * TC:(i // 2 + 1) * 2 * TC],
                                    lhsT=lhs[b:b + N_B, h // HPT, :],
                                    rhs=kaprho[d][b:b + N_B, h // HPT, :, :].rearrange("p x n -> p (x n)"),
                                    start=True, stop=True)
                        last.then_inc(crossed, 1)

                @block.scalar
                def _(act):
                    for n in range(6):
                        act.wait_ge(turned, n + 1)
                        act.activation(tok[n // 3][n % 3][:, :], ps[0:TC, n, :], ACT.Copy).then_inc(kept, 1)

                @block.vector
                def _(dve):
                    for g in range(4):
                        d, b0 = g // 2, 4 * (g % 2)
                        dve.wait_ge(crossed, g + 1)
                        for n in range(2):
                            both = ps[0:TC, b0 + 2 * n:b0 + 2 * n + 2, 0:4 * TC].rearrange(
                                "p b (i x q) -> p i b x q", i=2, x=2)
                            for x in range(2):
                                m = tri[:, 3 * d + (x or 2 * (n == 0)), None, :].to_broadcast([TC, G, TC]).rearrange(
                                    "p (i b) q -> p i b q", b=2)
                                dst = grams[g][2 * n + x][:, :, :].rearrange("p (i b) q -> p i b q", b=2)
                                dve.tensor_tensor(dst, both[:, :, :, x, :], m,
                                                  ALU.mult).then_inc(masked, 1)
                        dve.wait_ge(masked, 4 * g + 1)
                        dve.tensor_tensor(n_diag[g][:, :, :], grams[g][0][:, :, :],
                                          diag[:, None, 0:TC].to_broadcast([TC, G, TC]),
                                          ALU.mult).then_inc(n_cut, 1)

            names = [f"{n}{g}" for n in ("made", "copied", "grown", "grafted", "flipped", "level")
                     for g in range(4)]
            with k.stage(*names) as (block, *sems):
                made, copied, grown, grafted, flipped, level = [sems[4 * n:4 * n + 4] for n in range(6)]
                last_l = LEVELS1 - 1
                WIDE = TC // PACK * PACK
                grafts = lambda l: 3 * min(l, PACKED - 1) + max(l - PACKED + 1, 0)

                def bank(g, n):
                    return ps[0:TC, 2 * g + n, 0:G * TC].rearrange("p (i q) -> p i q", i=G)

                def bank_p(g, n):
                    return ps[0:TC, 2 * g + n, 0:G * PACK].rearrange("p (i q) -> p i q", i=G)

                @block.tensor
                def _(pe):
                    for l in range(LEVELS1):
                        for g in range(4):
                            if l:
                                pe.wait_ge(level[g], l + 3)
                            if 1 < l <= PACKED:
                                pe.wait_ge(grafted[g], grafts(l - 1))
                            for i in range(G):
                                if l == 0:
                                    out, lhs, rhs = bank_p(g, 0), n_diag[g], diag[:, TC:TC + PACK]
                                elif l < PACKED:
                                    out, lhs, rhs = bank_p(g, 0), n_diag[g], inv_p[g][:, i, :]
                                else:
                                    out, lhs, rhs = bank(g, 0), grams[g][0], inv[g][:, i, :]
                                last = pe.matmul(out[:, i, :], lhsT=lhs[:, i, :], rhs=rhs,
                                                 start=True, stop=True)
                            last.then_inc(made[g], 1)
                        if not l:
                            continue
                        for g in range(4):
                            pe.wait_ge(copied[g], l)
                            for i in range(G):
                                if l < PACKED:
                                    out, lhs, rhs = bank_p(g, 1), inv_t[g], nt_p[g]
                                elif l < last_l:
                                    out, lhs, rhs = bank(g, 1), inv_t[g], nt[g]
                                else:
                                    out, lhs, rhs = bank(g, 1), nt[g], inv_t[g]
                                last = pe.matmul(out[:, i, :], lhsT=lhs[:, i, :],
                                                 rhs=rhs[:, i, :], start=True, stop=True)
                            last.then_inc(grown[g], 1)
                        if l == last_l:
                            continue
                        for g in range(4):
                            pe.wait_ge(grafted[g], grafts(l) - (l < PACKED))
                            for i in range(G):
                                last = pe.transpose(bank(g, 0)[:, i, :], inv[g][:, i, :],
                                                    k.ident[0:TC, 0:TC])
                            last.then_inc(flipped[g], 1)

                @block.scalar
                def _(act):
                    for l in range(1, LEVELS1):
                        for g in range(4):
                            act.wait_ge(made[g], l + 1)
                            if l < PACKED:
                                act.activation(nt_p[g][:, :, :], bank_p(g, 0), ACT.Copy).then_inc(copied[g], 1)
                            else:
                                act.activation(nt[g][:, :, :], bank(g, 0), ACT.Copy).then_inc(copied[g], 1)
                        if l == last_l:
                            continue
                        for g in range(4):
                            act.wait_ge(flipped[g], l)
                            act.activation(inv_t[g][:, :, :], bank(g, 0), ACT.Copy).then_inc(level[g], 1)

                @block.vector
                def _(dve):
                    def graft(g, l, found, done):
                        d = g // 2
                        wide = lambda t: t.rearrange("p i (b q) -> p i b q", q=PACK)
                        dve.copy_predicated(
                            wide(inv[g][:, :, 0:WIDE]),
                            wide(masks[d][:, l, None, 0:WIDE].to_broadcast([TC, G, WIDE])),
                            found[:, :, None, :].to_broadcast([TC, G, WIDE // PACK, PACK])).then_inc(done, 1)
                        dve.copy_predicated(
                            inv[g][:, :, WIDE:TC],
                            masks[d][:, l, None, WIDE:TC].to_broadcast([TC, G, TC - WIDE]),
                            found[:, :, 0:TC - WIDE]).then_inc(done, 1)
                        dve.copy_predicated(
                            inv_p[g][:, :, :],
                            packed_masks[d][:, l, None, :].to_broadcast([TC, G, PACK]),
                            found).then_inc(done, 1)

                    for l in range(LEVELS1):
                        for g in range(4):
                            d = g // 2
                            m_inv = masks[d][:, l, None, :].to_broadcast([TC, G, TC])
                            m_inv_t = masks[1 - d][:, l, None, :].to_broadcast([TC, G, TC])
                            if l == 0:
                                dve.copy_predicated(inv_t[g][:, :, :], m_inv_t,
                                                    grams[g][0][:, :, :]).then_inc(level[g], 1)
                                dve.wait_ge(made[g], 1)
                                graft(g, l, bank_p(g, 0), level[g])
                            elif l < PACKED:
                                dve.wait_ge(grown[g], l)
                                graft(g, l, bank_p(g, 1), grafted[g])
                            elif l < last_l:
                                dve.wait_ge(grown[g], l)
                                dve.copy_predicated(inv[g][:, :, :], m_inv, bank(g, 1)
                                                    ).then_inc(grafted[g], 1)
                            else:
                                dve.wait_ge(grown[g], l)
                                dve.copy_predicated(inv_t[g][:, :, :], m_inv_t, bank(g, 1)
                                                    ).then_inc(level[g], 1)

            with k.stage("right", "right_kept", "solved", "u_kept", "out_made", "grown", "state_chain") as (
                    block, right, right_kept, solved, u_kept, out_made, grown, steps):
                @block.tensor
                def _(pe):
                    def place(h):
                        return N_B * (h % HPT), h // HPT, slice(h * N_B, (h + 1) * N_B)
                    for d in D2:
                        for h in range(H_B):
                            b, f, hs = place(h)
                            g, i = 2 * d + h // G, h % G
                            o = ps[0:TC, 2 * d + h % HPT, f * N_B:(f + 1) * N_B]
                            pe.matmul(o, lhsT=kaprho[d][b:b + N_B, f, 0, :],
                                      rhs=state[d][b:b + N_B, f, :], start=True, stop=False)
                            last = pe.matmul(o, lhsT=grams[g][2][:, i, :],
                                             rhs=tok[d][2][:, hs], start=False, stop=True)
                        last.then_inc(right, 1)
                    for d in D2:
                        pe.wait_ge(right_kept, d + 1)
                        for h in range(H_B):
                            b, f, hs = place(h)
                            last = pe.matmul(ps[0:TC, 4 + d, hs], lhsT=inv_t[2 * d + h // G][:, h % G, :],
                                             rhs=rn[d][:, hs], start=True, stop=True)
                        last.then_inc(solved, 1)
                    for d in D2:
                        pe.wait_ge(u_kept, d + 1)
                        for h in range(H_B):
                            b, f, hs = place(h)
                            g, i = 2 * d + h // G, h % G
                            o = ps[b:b + N_B, 6 + d, f * TC:(f + 1) * TC]
                            pe.matmul(o, lhsT=state[d][b:b + N_B, f, :],
                                      rhs=kaprho[d][b:b + N_B, f, 1, :], start=True, stop=False)
                            pe.matmul(o, lhsT=us[d][:, hs], rhs=grams[g][1][:, i, :], start=False, stop=False)
                            last = pe.matmul(o, lhsT=tok[d][2][:, hs], rhs=grams[g][3][:, i, :],
                                             start=False, stop=True)
                        last.then_inc(out_made, 1)
                        for h in range(H_B):
                            b, f, hs = place(h)
                            o = ps[b:b + N_B, d, f * N_B:(f + 1) * N_B]
                            pe.matmul(o, lhsT=tok[d][0][:, hs], rhs=us[d][:, hs], start=True, stop=False)
                            last = pe.matmul(o, lhsT=tok[d][1][:, hs], rhs=tok[d][2][:, hs],
                                             start=False, stop=True)
                        last.then_inc(grown, 1)

                @block.scalar
                def _(act):
                    for d in D2:
                        act.wait_ge(right, d + 1)
                        act.activation(rn[d][:, :].rearrange("p (f b n) -> p b f n", b=HPT, n=N_B),
                                       ps[0:TC, 2 * d:2 * d + 2, 0:RT * N_B].rearrange(
                                           "p b (f n) -> p b f n", n=N_B),
                                       ACT.Copy, scale=-1.0).then_inc(right_kept, 1)
                    for d in D2:
                        act.wait_ge(solved, d + 1)
                        act.activation(us[d][:, :], ps[0:TC, 4 + d, :], ACT.Copy).then_inc(u_kept, 1)

                @block.vector
                def _(dve):
                    chain = Chain(dve, steps)
                    for d in D2:
                        dve.wait_ge(out_made, d + 1)
                        chain(dve.tensor_tensor(cut(y, d), cut(y, d),
                                                ps[:, 6 + d, 0:RT * TC].rearrange("p (f n) -> p f n", f=RT),
                                                ALU.add))
                        dve.wait_ge(grown, d + 1)
                        chain(dve.tensor_tensor(state[d][:, :, :], state[d][:, :, :],
                                                ps[:, d, 0:RT * N_B].rearrange("p (f n) -> p f n", f=RT),
                                                ALU.add))
                        end = 0 if d else TC - 1
                        chain(dve.tensor_tensor(state[d][:, :, :], state[d][:, :, :],
                                                e_pos[d][:, :, end:end + 1].to_broadcast([P, RT, N_B]),
                                                ALU.mult))


def rwkv_out(k, r, key, v, rate, y, gate_in, s, sig):
    nc, ps = k.nc, k.ps
    bonus, t = sig[0], sig[1]
    with k.stage("bonus_chain") as (block, steps):
        @block.vector
        def _(dve):
            chain = Chain(dve, steps)
            chain(dve.tensor_tensor(s[:, :, :], rate[0][:, :, :], rate[1][:, :, :], ALU.add))
            for i in range(RT):
                chain(dve.tensor_scalar(s[:, i, :], s[:, i, :], -2.0, k.p1("k_a", i), ALU.add, ALU.mult))
                chain(dve.scalar_tensor_tensor(s[:, i, :], s[:, i, :], 2.0, key[:, i, :], ALU.add, ALU.mult))
                chain(dve.scalar_tensor_tensor(s[:, i, :], r[:, i, :], k.p1("r_k", i), s[:, i, :],
                                               ALU.mult, ALU.mult))
    tiles = [(("b", i), halves([(k.ones_h, s[:, i, :])])) for i in range(RT)]
    tiles += [(("m", i), halves([(k.ones_h, y[:, i, :])])) for i in range(RT)]

    def evac(dve, chain, key_, bank):
        kind, i = key_
        src = ps[:, bank:bank + 2, 0:HT]
        if kind == "b":
            return dve.tensor_tensor(split2(bonus[:, i, :]), src, split2(v[:, i, :]), ALU.mult)
        return dve.scalar_tensor_tensor(split2(y[:, i, :]), src, -1.0 / N_B, split2(y[:, i, :]),
                                        ALU.mult, ALU.add)
    linear(k, "bonus", [([], tiles)], evac)
    rms_scale(k, "gn", [[y[:, i, :]] for i in range(RT)], float(N_B), k.ones_h, "gn", s, t)
    with k.stage("gn_chain") as (block, steps):
        @block.vector
        def _(dve):
            chain = Chain(dve, steps)
            for i in range(RT):
                chain(dve.scalar_tensor_tensor(y[:, i, :], y[:, i, :], k.p1("gn_g", i), t[:, i, :],
                                               ALU.mult, ALU.mult))
                chain(dve.scalar_tensor_tensor(y[:, i, :], y[:, i, :], k.p1("gn_b", i), bonus[:, i, :],
                                               ALU.add, ALU.add))
    tiles = [(i, halves([(k.g2[:, i * P:(i + 1) * P], gate_in)])) for i in range(RT)]
    linear(k, "gate", [([], tiles)], lambda dve, ch, i, bank: dve.tensor_tensor(
        split2(y[:, i, :]), ps[:, bank:bank + 2, 0:HT], split2(y[:, i, :]), ALU.mult))


def mix_out(k, a, li, y):
    nc, ps = k.nc, k.ps
    with ExitStack() as tmp:
        ring = [k.sb(f"wout{i}", [P, KD, 256], stack=tmp) for i in range(2)]
        w = a["w_out"][bass.ds(li, 1), :, :].rearrange("a (t p) n -> p (a t) n", p=P)
        x = [k.att[:, i, :] for i in range(4)] + [y[:, i, :] for i in range(RT)]
        strips = []
        for s in range(4):
            buf = ring[s % 2]
            strips.append(([(buf[:, :, :], w[:, :, s * 256:(s + 1) * 256])],
                           [(2 * s + m, halves([(buf[:, i, m * P:(m + 1) * P], x[i]) for i in range(KD)]))
                            for m in range(2)]))
        linear(k, "w_out", strips, lambda dve, ch, m, bank: dve.scalar_tensor_tensor(
            split2(k.h[:, m, :]), split2(k.h[:, m, :]), ALPHA, ps[:, bank:bank + 2, 0:HT],
            ALU.mult, ALU.add))
        with ExitStack() as ln:
            st = k.sb("ln_st", [P, T], stack=ln)
            g, b = COL1["ln1_g"], COL1["ln1_b"]
            layer_norm(k, k.h, k.par1[:, g:g + KD], k.par1[:, b:b + KD], k.h, k.u[:, 0:KD, :], st[:, :])


def moe(k, a, li):
    nc, ps = k.nc, k.ps
    NR = GROUPS + EXPERTS
    with ExitStack() as tmp:
        def sb(name, shape, dt=F32):
            return k.sb(name, shape, dt, stack=tmp)
        gate = sb("gate", [TC, 2, NC1])
        dest = sb("dest", [TC, 2, NC1], I32)
        slots = sb("slots", [SLOT, NBLK + 1], I32)
        owner = sb("owner", [1, NBLK], I32)
        pairs = sb("pairs", [1, 1], I32)
        with ExitStack() as rt:
            route(k, a, li, rt, gate, dest, slots, owner, pairs, NR)
        with ExitStack() as ex:
            experts(k, a, li, ex, slots, owner, pairs)
        with ExitStack() as cb:
            combine(k, cb, gate, dest)
    with ExitStack() as ln:
        st = k.sb("ln2_st", [P, T], stack=ln)
        sc = k.sb("ln2_sc", [P, KD, T], stack=ln)
        g, b = COL1["ln2_g"], COL1["ln2_b"]
        layer_norm(k, k.h, k.par1[:, g:g + KD], k.par1[:, b:b + KD], k.h, sc, st[:, :])


def route(k, a, li, rt, gate, dest, slots, owner, pairs, NR):
    nc, ps = k.nc, k.ps

    def sb(name, shape, dt=F32):
        return k.sb(name, shape, dt, stack=rt)
    w = sb("router", [P, KD, NR])
    wb = sb("router_b", [1, NR])
    rows = sb("h_rows_sb", [TC, NC1, D])
    lg = sb("logits", [TC, NC1, NR])
    tri = sb("before", [TC, TC])
    iota = sb("iota", [TC, 64])
    tok = sb("tok_id", [TC, NC1], I32)
    with k.stage("router_landed", "logits_made", "h_turned", "h_kept", "h_stored", "lg_chain") as (
            block, landed, made, turned, kept, stored, steps):
        @block.sync
        def _(sp):
            sp.dma_start(w[:, :, :], a["router"][bass.ds(li, 1), :, :].rearrange(
                "a (t p) n -> p (a t) n", p=P)).then_inc(landed, 16)
            sp.dma_start(wb[:, :], a["router_b"][bass.ds(li, 1), :]).then_inc(landed, 16)
            sp.dma_start(tri[:, :], a["k_tri"][:, 0, :]).then_inc(landed, 16)
            sp.dma_start(iota[:, :], a["k_iota"]).then_inc(landed, 16)
            sp.dma_start(tok[:, :], a["k_tok"]).then_inc(landed, 16)
            for j in range(NC1):
                sp.wait_ge(kept, j + 1)
                sp.dma_start(k.h_rows[j * TC:(j + 1) * TC, :], rows[:, j, :]).then_inc(stored, 16)
            sp.wait_ge(stored, 16 * NC1)

        @block.tensor
        def _(pe):
            for j in range(NC1):
                if j >= 3:
                    pe.wait_ge(kept, j - 2)
                for f in range(KD):
                    last = pe.transpose(ps[0:TC, 2 * (j % 3) + f // 4, (f % 4) * P:(f % 4 + 1) * P],
                                        k.h[:, f, j * TC:(j + 1) * TC], k.ident)
                last.then_inc(turned, 1)
            pe.wait_ge(landed, 16 * 5)
            for j in range(NC1):
                o = ps[0:TC, 6, j * NR:(j + 1) * NR]
                for f in range(KD):
                    pe.matmul(o, lhsT=k.h[:, f, j * TC:(j + 1) * TC], rhs=w[:, f, :],
                              start=(f == 0), stop=False)
                last = pe.matmul(o, lhsT=k.ones[0:1, 0:TC], rhs=wb[:, :], start=False, stop=True)
            last.then_inc(made, 1)

        @block.scalar
        def _(act):
            for j in range(NC1):
                act.wait_ge(turned, j + 1)
                b = 2 * (j % 3)
                act.activation(rows[:, j, :].rearrange("p (a b) -> p a b", a=2), ps[0:TC, b:b + 2, :],
                               ACT.Copy).then_inc(kept, 1)

        @block.vector
        def _(dve):
            dve.wait_ge(made, 1)
            dve.tensor_copy(lg[:, :, :], ps[0:TC, 6, 0:NC1 * NR].rearrange(
                "p (j n) -> p j n", j=NC1)).then_inc(steps, 1)

    big = 1000.0
    gp = sb("g_prob", [TC, NC1, GROUPS])
    ep = sb("e_prob", [TC, NC1, PER_GROUP])
    t8 = sb("t8", [TC, NC1, PER_GROUP])
    one = sb("one", [TC, 8, NC1, 1])
    ohg = sb("oh_group", [TC, NC1, GROUPS])
    oh = [sb(f"oh{n}", [TC, NC1, PER_GROUP]) for n in range(2)]
    both = [sb(f"assigned{n}", [TC, NC1, EXPERTS]) for n in range(2)]
    count = sb("count", [TC, NC1, EXPERTS])
    t32 = sb("t32", [TC, NC1, EXPERTS])
    total = sb("total", [TC, EXPERTS])
    nb = sb("n_blocks", [TC, EXPERTS])
    pend = sb("pend", [TC, EXPERTS])
    ones32 = sb("ones32", [TC, EXPERTS])
    own = sb("own", [1, NBLK, EXPERTS])
    ownf = sb("ownf", [1, NBLK])
    pf = sb("pairs_f", [1, NBLK // 2])
    with k.stage("g_shifted", "g_exp", "e_shifted", "e_exp", "counted", "ranked", "dest_made",
                 "scattered", "slots_in", "tail_set", "route_chain") as (
            block, g_sh, g_ex, e_sh, e_ex, counted, ranked, dest_made, scattered, slots_in, tail_set, steps):

        def wide(x, n):
            return x.to_broadcast([TC, NC1, n])

        @block.scalar
        def _(act):
            act.wait_ge(g_sh, 1)
            act.activation(gp[:, :, :], gp[:, :, :], ACT.Exp).then_inc(g_ex, 1)
            act.wait_ge(e_sh, 1)
            act.activation(ep[:, :, :], ep[:, :, :], ACT.Exp).then_inc(e_ex, 1)

        @block.tensor
        def _(pe):
            pe.wait_ge(counted, 1)
            for j in range(NC1):
                for i in range(j + 1):
                    pe.matmul(ps[0:TC, 0, j * EXPERTS:(j + 1) * EXPERTS],
                              lhsT=tri[:, :] if i == j else k.ones[0:TC, 0:TC],
                              rhs=count[:, i, :], start=(i == 0), stop=(i == j))
            for i in range(NC1):
                last = pe.matmul(ps[0:TC, 1, 0:EXPERTS], lhsT=k.ones[0:TC, 0:TC], rhs=count[:, i, :],
                                 start=(i == 0), stop=(i == NC1 - 1))
            last.then_inc(ranked, 1)

        @block.gpsimd
        def _(gpo):
            gpo.wait_ge(k.y_cleared, 16)
            gpo.memset(slots[:, NBLK:NBLK + 1], 0).then_inc(tail_set, 1)
            gpo.wait_ge(dest_made, 1)
            for n in range(2):
                for j in range(NC1):
                    gpo.indirect_dma_start(
                        out=k.row_tok[:, :], out_offset=bass.IndirectOffsetOnAxis(
                            ap=dest[:, n, j:j + 1].bitcast(U32), axis=0),
                        in_=tok[:, j:j + 1], in_offset=None).then_inc(scattered, 16)
            gpo.wait_ge(scattered, 16 * 2 * NC1)

        @block.sync
        def _(sp):
            sp.wait_ge(scattered, 16 * 2 * NC1)
            sp.dma_start(slots[:, 0:NBLK], k.row_tok.rearrange("(b s) o -> s (b o)", s=SLOT),
                         allow_slow_non_contiguous=True).then_inc(slots_in, 16)
            sp.wait_ge(slots_in, 16)

        @block.vector
        def _(dve):
            chain = Chain(dve, steps)

            def pick(src, n, top, hot):
                t = t8[:, :, 0:n]
                io = iota[:, None, 0:n].to_broadcast([TC, NC1, n])
                chain(dve.tensor_reduce(top, src, AX.X, ALU.max))
                chain(dve.tensor_tensor(t, src, wide(top, n), ALU.is_equal))
                chain(dve.scalar_tensor_tensor(t, t, -big, io, ALU.mult, ALU.add))
                chain(dve.tensor_reduce(one[:, 7, :, :], t, AX.X, ALU.min))
                chain(dve.tensor_tensor(hot, t, wide(one[:, 7, :, :], n), ALU.is_equal))

            def softmax(src, dst, n, made, done):
                chain(dve.tensor_reduce(one[:, 0, :, :], src, AX.X, ALU.max))
                dve.tensor_tensor(dst, src, wide(one[:, 0, :, :], n), ALU.subtract).then_inc(made, 1)
                dve.wait_ge(done, 1)
                chain(dve.tensor_reduce(one[:, 0, :, :], dst, AX.X, ALU.add))
                chain(dve.reciprocal(one[:, 0, :, :], one[:, 0, :, :]))
                chain(dve.tensor_tensor(dst, dst, wide(one[:, 0, :, :], n), ALU.mult))

            softmax(lg[:, :, 0:GROUPS], gp[:, :, :], GROUPS, g_sh, g_ex)
            pick(gp[:, :, :], GROUPS, one[:, 1, :, :], ohg[:, :, :])
            el = lg[:, :, GROUPS:].rearrange("p j (g e) -> p j g e", g=GROUPS)
            for g in range(GROUPS):
                h1 = wide(ohg[:, :, g:g + 1], PER_GROUP)
                if g == 0:
                    chain(dve.tensor_tensor(ep[:, :, :], el[:, :, g, :], h1, ALU.mult))
                else:
                    chain(dve.tensor_tensor(t8[:, :, :], el[:, :, g, :], h1, ALU.mult))
                    chain(dve.tensor_tensor(ep[:, :, :], ep[:, :, :], t8[:, :, :], ALU.add))
            softmax(ep[:, :, :], ep[:, :, :], PER_GROUP, e_sh, e_ex)
            for n in range(2):
                pick(ep[:, :, :], PER_GROUP, one[:, 2 + n, :, :], oh[n][:, :, :])
                chain(dve.tensor_tensor(gate[:, n, :], one[:, 1, :, 0], one[:, 2 + n, :, 0], ALU.mult))
                if n == 0:
                    chain(dve.scalar_tensor_tensor(ep[:, :, :], oh[0][:, :, :], -2.0, ep[:, :, :],
                                                   ALU.mult, ALU.add))
                shape = [TC, NC1, GROUPS, PER_GROUP]
                chain(dve.tensor_tensor(both[n][:, :, :].rearrange("p j (g e) -> p j g e", g=GROUPS),
                                        ohg[:, :, :, None].to_broadcast(shape),
                                        oh[n][:, :, None, :].to_broadcast(shape), ALU.mult))
            dve.tensor_tensor(count[:, :, :], both[0][:, :, :], both[1][:, :, :], ALU.add).then_inc(counted, 1)
            dve.wait_ge(ranked, 1)
            chain(dve.tensor_copy(total[:, :], ps[0:TC, 1, 0:EXPERTS]))
            chain(dve.tensor_scalar(nb[:, :], total[:, :], 0.0, None, ALU.is_gt))
            for m in range(1, -(-T // SLOT)):
                chain(dve.scalar_tensor_tensor(nb[:, :], total[:, :], float(m * SLOT), nb[:, :],
                                               ALU.is_gt, ALU.add))
            chain(dve.memset(ones32[:, :], 1.0))
            chain(dve.tensor_tensor_scan(pend[:, :], ones32[:, :], nb[:, :], 0.0, ALU.mult, ALU.add))
            chain(dve.tensor_tensor(nb[:, :], pend[:, :], nb[:, :], ALU.subtract))
            chain(dve.tensor_scalar(nb[:, :], nb[:, :], float(SLOT), None, ALU.mult))
            chain(dve.tensor_tensor(t32[:, :, :], ps[0:TC, 0, 0:NC1 * EXPERTS].rearrange(
                "p (j e) -> p j e", j=NC1), nb[:, None, :].to_broadcast([TC, NC1, EXPERTS]), ALU.add))
            for n in range(2):
                chain(dve.tensor_tensor(both[n][:, :, :], both[n][:, :, :], t32[:, :, :], ALU.mult))
                chain(dve.tensor_reduce(one[:, 4 + n, :, :], both[n][:, :, :], AX.X, ALU.add))
                chain(dve.tensor_copy(dest[:, n, :], one[:, 4 + n, :, 0]))
            dve.nop().then_inc(dest_made, 1)
            chain(dve.tensor_tensor(own[:, :, :], pend[0:1, None, :].to_broadcast([1, NBLK, EXPERTS]),
                                    iota[0:1, 0:NBLK, None].to_broadcast([1, NBLK, EXPERTS]), ALU.is_le))
            chain(dve.tensor_reduce(ownf[:, :], own[:, :, :], AX.X, ALU.add))
            chain(dve.tensor_scalar(owner[:, :], ownf[:, :], float(EXPERTS - 1), None, ALU.min))
            even = iota[0:1, 0:NBLK].rearrange("p (a b) -> p a b", b=2)[:, :, 0]
            chain(dve.tensor_scalar(pf[:, :], even, pend[0:1, EXPERTS - 1:EXPERTS], None, ALU.is_lt))
            chain(dve.tensor_reduce(ownf[:, 0:1], pf[:, :], AX.X, ALU.add))
            chain(dve.tensor_copy(pairs[:, :], ownf[:, 0:1]))


def experts(k, a, li, ex, slots, owner, pairs):
    nc, ps = k.nc, k.ps
    Z = range(2)

    def sb(name, shape, dt=F32):
        return k.sb(name, shape, dt, stack=ex)
    w1 = [sb(f"e_w1{z}", [P, KD, EH]) for z in Z]
    w3 = [sb(f"e_w3{z}", [P, KD, EH]) for z in Z]
    w2 = [sb(f"e_w2{z}", [P, 2, D]) for z in Z]
    x = [sb(f"e_x{z}", [SLOT, D]) for z in Z]
    xt = [sb(f"e_xt{z}", [P, KD, SLOT]) for z in Z]
    si = [sb(f"e_silu{z}", [P, 2, SLOT]) for z in Z]
    hid = [sb(f"e_hid{z}", [P, 2, SLOT]) for z in Z]
    y = [sb(f"e_y{z}", [SLOT, D]) for z in Z]
    idx = [sb(f"e_idx{z}", [SLOT, 1], I32) for z in Z]
    d1 = a["moe_w1"].rearrange("l e (t p) n -> (l e) p t n", p=P)
    d3 = a["moe_w3"].rearrange("l e (t p) n -> (l e) p t n", p=P)
    d2 = a["moe_w2"].rearrange("l e (t p) n -> (l e) p t n", p=P)
    names = ["up_w", "down_w", "idx_set", "x_in", "x_turned", "x_kept", "up", "silu", "hidden",
             "down", "y_kept", "y_out"]
    with k.stage("passed_gp", "passed_pe", "passed_act", *[f"{n}{z}" for n in names for z in Z]) as (
            block, passed_gp, passed_pe, passed_act, *sems):
        (up_w, down_w, idx_set, x_in, x_turned, x_kept, up, silu, hidden, down, y_kept,
         y_out) = [sems[2 * i:2 * i + 2] for i in range(len(names))]

        def turns(eng):
            return eng.Fori(0, eng.value_load(pairs[0:1, 0:1], min_val=1, max_val=NBLK // 2))

        def credit(eng, *released):
            for s in released:
                for z in Z:
                    eng.sem_inc(s[z], 1)

        @block.sync
        def _(sp):
            sp.wait_ge(k.y_cleared, 16)
            with turns(sp) as i:
                for z in Z:
                    e = sp.value_load(owner[0:1, bass.ds(2 * i + z, 1)], min_val=0, max_val=EXPERTS - 1)
                    row = li * EXPERTS + e
                    one = lambda d: d[bass.ds(row, 1), :, :, :].rearrange("a p t n -> (a p) t n")
                    sp.wait_ge(up[z], i + 1)
                    sp.dma_start(w1[z][:, :, :], one(d1)).then_inc(up_w[z], 16)
                    sp.dma_start(w3[z][:, :, :], one(d3)).then_inc(up_w[z], 16)
                    sp.wait_ge(down[z], i + 1)
                    sp.dma_start(w2[z][:, :, :], one(d2)).then_inc(down_w[z], 16)

        def fetch(gp, z):
            gp.indirect_dma_start(
                out=x[z][:, :], out_offset=None, in_=k.h_rows[:, :],
                in_offset=bass.IndirectOffsetOnAxis(ap=idx[z][:, 0:1].bitcast(U32), axis=0)
            ).then_inc(x_in[z], 16)

        @block.gpsimd
        def _(gp):
            gp.tensor_copy(idx[0][:, :], slots[:, 0:1]).then_inc(idx_set[0], 1)
            gp.wait_ge(idx_set[0], 1)
            fetch(gp, 0)
            with turns(gp) as i:
                for z, column, freed, count in ((1, 2 * i + 1, i + 1, i + 1), (0, 2 * i + 2, i + 2, i + 2)):
                    gp.wait_ge(x_turned[z], freed)
                    gp.tensor_copy(idx[z][:, :], slots[:, bass.ds(column, 1)]).then_inc(idx_set[z], 1)
                    gp.wait_ge(idx_set[z], count)
                    gp.sem_inc(passed_gp, 1)
                    fetch(gp, z)

        @block.tensor
        def _(pe):
            credit(pe, x_turned, up, down)

            def turn_rows(z):
                for f in range(KD):
                    last = pe.transpose(ps[:, z, f * SLOT:(f + 1) * SLOT],
                                        x[z][:, f * P:(f + 1) * P], k.ident[0:SLOT, 0:SLOT])
                last.then_inc(x_turned[z], 1)

            pe.wait_ge(x_in[0], 16)
            turn_rows(0)
            with turns(pe) as i:
                for z in Z:
                    pe.wait_ge(x_kept[z], i + 2)
                    pe.wait_ge(up_w[z], i * 32 + 32)
                    pe.wait_ge(hidden[z], i + 1)
                    for n, w in enumerate((w1[z], w3[z])):
                        for m in range(2):
                            o = ps[:, 2 + z, (2 * n + m) * SLOT:(2 * n + m + 1) * SLOT]
                            for f in range(KD):
                                last = pe.matmul(o, lhsT=w[:, f, m * P:(m + 1) * P], rhs=xt[z][:, f, :],
                                                 start=(f == 0), stop=(f == KD - 1))
                    last.then_inc(up[z], 1)
                    pe.wait_ge(x_in[1 - z], i * 16 + (32 if z else 16))
                    pe.wait_ge(x_kept[1 - z], i + (2 if z else 1))
                    pe.sem_inc(passed_pe, 1)
                    turn_rows(1 - z)
                    pe.wait_ge(hidden[z], i + 2)
                    pe.wait_ge(down_w[z], i * 16 + 16)
                    pe.wait_ge(y_kept[z], i + 1)
                    for c in range(2):
                        for t in range(2):
                            last = pe.matmul(ps[0:SLOT, 4 + 2 * z + c, :], lhsT=hid[z][:, t, :],
                                             rhs=w2[z][:, t, c * 512:(c + 1) * 512],
                                             start=(t == 0), stop=(t == 1))
                    last.then_inc(down[z], 1)

        @block.scalar
        def _(act):
            credit(act, x_kept)
            for z in Z:
                act.sem_inc(y_out[z], 16)

            def keep_rows(z):
                act.activation(xt[z][:, :, :], ps[:, z, :].rearrange("p (f n) -> p f n", f=KD),
                               ACT.Copy).then_inc(x_kept[z], 1)

            act.wait_ge(x_turned[0], 2)
            keep_rows(0)
            n_turns = act.value_load(pairs[0:1, 0:1], min_val=1, max_val=NBLK // 2)
            with act.Fori(0, n_turns) as i:
                for z in Z:
                    act.wait_ge(up[z], i + 2)
                    act.wait_ge(hidden[z], i + 1)
                    act.activation(si[z][:, :, :], ps[:, 2 + z, 0:2 * SLOT].rearrange(
                        "p (m n) -> p m n", m=2), ACT.Silu).then_inc(silu[z], 1)
                    act.wait_ge(x_turned[1 - z], i + (3 if z else 2))
                    act.wait_ge(up[1 - z], i + (2 if z else 1))
                    keep_rows(1 - z)
                for z in Z:
                    act.wait_ge(y_kept[z], i + 2)
                    act.dma_start(k.y_rows[bass.ds((2 * i + z) * SLOT, SLOT), :], y[z][:, :]
                                  ).then_inc(y_out[z], 16)
            for z in Z:
                act.wait_ge(y_out[z], n_turns * 16 + 16)
            act.sem_inc(passed_act, 1)

        @block.vector
        def _(dve):
            credit(dve, hidden, y_kept)
            with turns(dve) as i:
                for z in Z:
                    dve.wait_ge(silu[z], i + 1)
                    dve.wait_ge(down[z], i + 1)
                    dve.tensor_tensor(hid[z][:, :, :], ps[:, 2 + z, 2 * SLOT:4 * SLOT].rearrange(
                        "p (m n) -> p m n", m=2), si[z][:, :, :], ALU.mult).then_inc(hidden[z], 1)
                    dve.wait_ge(down[z], i + 2)
                    dve.wait_ge(y_out[z], i * 16 + 16)
                    dve.tensor_copy(y[z][:, :].rearrange("p (a b) -> p a b", a=2),
                                    ps[0:SLOT, 4 + 2 * z:6 + 2 * z, :]).then_inc(y_kept[z], 1)


def combine(k, cb, gate, dest):
    nc, ps = k.nc, k.ps
    y = k.sb("c_y", [TC, 2, 2, D], stack=cb)
    with k.stage("y0_in", "y1_in", "weighted", "c_turned", "c_added", "c_chain") as (
            block, in0, in1, weighted, turned, added, steps):
        landed = (in0, in1)

        @block.gpsimd
        def _(gp):
            for j in range(NC1):
                if j >= 2:
                    gp.wait_ge(turned, j - 1)
                for n in range(2):
                    gp.indirect_dma_start(
                        out=y[:, j % 2, n, :], out_offset=None, in_=k.y_rows[:, :],
                        in_offset=bass.IndirectOffsetOnAxis(ap=dest[:, n, j:j + 1].bitcast(U32), axis=0)
                    ).then_inc(landed[j % 2], 16)

        @block.vector
        def _(dve):
            chain = Chain(dve, steps)
            for j in range(NC1 + 1):
                if j < NC1:
                    z = j % 2
                    dve.wait_ge(landed[z], 32 * (j // 2 + 1))
                    chain(dve.tensor_scalar(y[:, z, 0, :], y[:, z, 0, :], gate[:, 0, j:j + 1], None, ALU.mult))
                    dve.scalar_tensor_tensor(y[:, z, 0, :], y[:, z, 1, :], gate[:, 1, j:j + 1],
                                             y[:, z, 0, :], ALU.mult, ALU.add).then_inc(weighted, 1)
                if j >= 1:
                    i = j - 1
                    dve.wait_ge(turned, i + 1)
                    b = 2 * (i % 2)
                    ht = k.h[:, :, i * TC:(i + 1) * TC]
                    for c in range(2):
                        last = dve.scalar_tensor_tensor(
                            ht[:, 4 * c:4 * c + 4, :], ht[:, 4 * c:4 * c + 4, :], ALPHA,
                            ps[:, b + c, 0:4 * TC].rearrange("p (f n) -> p f n", f=4), ALU.mult, ALU.add)
                        if c == 0:
                            last.then_inc(steps, 1)
                            chain.n += 1
                    last.then_inc(added, 1)
                    dve.wait_ge(added, i + 1)

        @block.tensor
        def _(pe):
            for j in range(NC1):
                pe.wait_ge(weighted, j + 1)
                if j >= 2:
                    pe.wait_ge(added, j - 1)
                for f in range(KD):
                    last = pe.transpose(ps[:, 2 * (j % 2) + f // 4, (f % 4) * TC:(f % 4 + 1) * TC],
                                        y[:, j % 2, 0, f * P:(f + 1) * P], k.ident[0:TC, 0:TC])
                last.then_inc(turned, 1)


def modulated_norm(k, name, tiles, cols, gain, shift, out, sq, st):
    rms_scale(k, name, [tiles], D, k.ones[:, :], "rms", sq, st)
    with k.stage(f"{name}_scaled", f"{name}_shifted") as (block, scaled, shifted):
        @block.vector
        def _(dve):
            for f in range(KD):
                dve.scalar_tensor_tensor(out[f], tiles[f], gain(f), st[:, 0, 0:cols], ALU.mult,
                                         ALU.mult).then_inc(scaled, 1)

        if shift is not None:
            @block.scalar
            def _(act):
                for f in range(KD):
                    act.wait_ge(scaled, f + 1)
                    act.activation(out[f], out[f], ACT.Identity, bias=shift(f)).then_inc(shifted, 1)


def second_block(k, a):
    nc, ps = k.nc, k.ps
    x = [k.h[:, f, META:T] for f in range(KD)]
    w_in = a["w_in_2"][0].rearrange("(t p) n -> p t n", p=P)
    with ExitStack() as s2:
        mod = k.sb("mod", [P, 6 * KD, 2], stack=s2)
        gain = k.sb("gain", [P, 3, KD], stack=s2)
        hl = k.sb("h_lat", [P, KD, SEQ], stack=s2)
        with ExitStack() as mix:
            ys = [k.sb(f"y_branch{n}", [P, 4, SEQ], stack=mix) for n in range(3)]
            hc = k.sb("h_ctx", [P, KD, CTX], stack=mix)
            modulation(k, a, mod, gain)
            load_context(k, a, hc)
            with ExitStack() as t:
                sq = k.sb("n_sq", [P, KD, SEQ], stack=t)
                st = k.sb("n_st", [P, 1, SEQ], stack=t)
                modulated_norm(k, "lat", x, SEQ, lambda f: gain[:, 0, f:f + 1],
                               lambda f: mod[:, f, 0:1], [hl[:, f, :] for f in range(KD)], sq, st)
                modulated_norm(k, "ctx", [hc[:, f, :] for f in range(KD)], CTX,
                               lambda f: gain[:, 1, f:f + 1], lambda f: mod[:, f, 1:2],
                               [hc[:, f, :] for f in range(KD)], sq, st)
            with ExitStack() as at:
                attend(k, a, at, w_in, hl, hc, ys)
            with ExitStack() as gl:
                gated_linear(k, a, gl, w_in, hl, hc, ys[2])
            with ExitStack() as mg:
                merge(k, a, mg, w_in, hl, ys, mod, x)
        with ExitStack() as t:
            sq = k.sb("f_sq", [P, KD, SEQ], stack=t)
            st = k.sb("f_st", [P, 1, SEQ], stack=t)
            modulated_norm(k, "ffn", x, SEQ, lambda f: gain[:, 2, f:f + 1],
                           lambda f: mod[:, 3 * KD + f, 0:1], [hl[:, f, :] for f in range(KD)], sq, st)
        with ExitStack() as ff:
            feed_forward(k, a, ff, hl, gain, mod, x)
        with ExitStack() as t:
            sq = k.sb("o_sq", [P, KD, SEQ], stack=t)
            st = k.sb("o_st", [P, 1, SEQ], stack=t)
            finish(k, a, hl, x, sq, st)


def modulation(k, a, mod, gain):
    nc, ps = k.nc, k.ps
    w = a["w_mod_2"][0].rearrange("(t p) n -> p t n", p=P)
    with ExitStack() as t:
        c = k.sb("c_silu", [P, KD, 2], stack=t)
        ring = [k.sb(f"wmod{i}", [P, KD, 512], stack=t) for i in range(2)]
        with k.stage("c_done") as (block, done):
            @block.scalar
            def _(act):
                c0 = COL2["c"]
                act.activation(c[:, :, :], k.par2[:, c0:c0 + 2 * KD].rearrange("p (v t) -> p t v", v=2),
                               ACT.Silu).then_inc(done, 1)
        strips = []
        for s in range(12):
            buf = ring[s % 2]
            strips.append(([(buf[:, :, :], w[:, :, s * 512:(s + 1) * 512])],
                           [(4 * s + m, [(0, 2, P, [(buf[:, i, m * P:(m + 1) * P], c[:, i, :])
                                                    for i in range(KD)])]) for m in range(4)]))
        linear(k, "w_mod", strips, lambda dve, ch, m, bank: dve.tensor_scalar(
            mod[:, m, :], ps[:, bank, 0:2], k.p2("b_mod", m), None, ALU.add))
    with k.stage("gain_done") as (block, done):
        @block.vector
        def _(dve):
            for n, (j, which, g) in enumerate(((1, 0, "norm_mix"), (1, 1, "norm_mix"), (4, 0, "norm_ffn"))):
                c0 = COL2[g]
                dve.scalar_tensor_tensor(gain[:, n, :], mod[:, j * KD:(j + 1) * KD, which], 1.0,
                                         k.par2[:, c0:c0 + KD], ALU.add, ALU.mult).then_inc(done, 1)


def load_context(k, a, hc):
    nc, ps = k.nc, k.ps
    with ExitStack() as t:
        rows = k.sb("ctx_rows", [P, CT, D], stack=t)
        with k.stage("ctx_landed", "ctx_turned", "ctx_kept") as (block, landed, turned, kept):
            @block.sync
            def _(sp):
                sp.dma_start(rows[:, :, :], a["ctx_2"][0].rearrange("(j p) n -> p j n", p=P)
                             ).then_inc(landed, 16)

            @block.tensor
            def _(pe):
                pe.wait_ge(landed, 16)
                for j in range(CT):
                    for f in range(KD):
                        last = pe.transpose(ps[:, 2 * j + f // 4, (f % 4) * P:(f % 4 + 1) * P],
                                            rows[:, j, f * P:(f + 1) * P], k.ident)
                    last.then_inc(turned, 1)

            @block.scalar
            def _(act):
                for j in range(CT):
                    act.wait_ge(turned, j + 1)
                    for c in range(2):
                        act.activation(hc[:, 4 * c:4 * c + 4, j * P:(j + 1) * P],
                                       ps[:, 2 * j + c, :].rearrange("p (f n) -> p f n", f=4),
                                       ACT.Copy).then_inc(kept, 1)


def attend(k, a, at, w_in, hl, hc, ys):
    nc, ps = k.nc, k.ps
    HD, W = 64, CTX + SEQ

    def sb(name, shape):
        return k.sb(name, shape, stack=at)
    q = [sb(f"q_{n}", [P, 4, SEQ]) for n in "ab"]
    kt = [sb(f"k_{n}", [P, 2, W]) for n in "ab"]
    v = sb("v_ab", [P, ST, 256])
    with ExitStack() as t:
        ring = [k.sb(f"wab{i}", [P, KD, 512], stack=t) for i in range(2)]

        def feat(buf, m, src):
            n = src.shape[-1]
            return [(0, n, P, [(buf[:, i, m * P:(m + 1) * P], src[:, i, :]) for i in range(KD)])]

        def toks(buf, j):
            src, o = (hc, j) if j < CT else (hl, j - CT)
            return [(0, 256, P, [(src[:, i, o * P:(o + 1) * P], buf[:, i, 0:256]) for i in range(KD)])]
        k_loads = [(ring[1][:, :, (4 * n + 2 * g + c) * HD:(4 * n + 2 * g + c + 1) * HD],
                    w_in[:, :, c0 + g * HD:c0 + (g + 1) * HD])
                   for n, c0 in enumerate((512, 1280)) for g in range(2) for c in range(2)]
        strips = [
            ([(ring[0][:, :, :], w_in[:, :, 0:512])],
             [(("q", 0, m), feat(ring[0], m, hl)) for m in range(4)]),
            (k_loads, [(("k", n, g, c), feat(ring[1], 2 * n + g, (hc, hl)[c]))
                       for n in range(2) for g in range(2) for c in range(2)]),
            ([(ring[0][:, :, :], w_in[:, :, 768:1280])],
             [(("q", 1, m), feat(ring[0], m, hl)) for m in range(4)]),
            ([(ring[1][:, :, 0:128], w_in[:, :, 640:768]), (ring[1][:, :, 128:256], w_in[:, :, 1408:1536])],
             [(("v", j), toks(ring[1], j)) for j in range(ST)])]

        def evac(dve, chain, key, bank):
            if key[0] == "q":
                return dve.tensor_copy(q[key[1]][:, key[2], :], ps[:, bank, :])
            if key[0] == "v":
                return dve.tensor_copy(v[:, key[1], :], ps[:, bank, 0:256])
            _, n, g, c = key
            dst = kt[n][:, g, CTX:W] if c else kt[n][:, g, 0:CTX]
            return dve.tensor_copy(dst, ps[:, bank, 0:dst.shape[-1]])
        linear(k, "ab", strips, evac)
    with ExitStack() as t:
        sq = k.sb("ab_sq", [P, 4, SEQ], stack=t)
        st = k.sb("ab_st", [P, 4, SEQ], stack=t)
        table = k.sb("table", [P, 2, SEQ], stack=t)
        with k.stage("table_in") as (block, landed):
            @block.sync
            def _(sp):
                sp.dma_start(table[:, :, :], a["k_axial"]).then_inc(landed, 16)
                sp.wait_ge(landed, 16)
        for name, tiles, g in (("bq", [q[1][:, m, :] for m in range(4)], "qn"),
                               ("bk", [kt[1][:, m, CTX:W] for m in range(2)], "kn"),
                               ("bkc", [kt[1][:, m, 0:CTX] for m in range(2)], "kn")):
            n = tiles[0].shape[-1]
            rms_scale(k, name, [[x] for x in tiles], float(HD), k.ones_h, "rms", sq, st)
            with k.stage(f"{name}_normed") as (block, normed):
                @block.vector
                def _(dve):
                    for m, x in enumerate(tiles):
                        dve.scalar_tensor_tensor(x, x, k.p2(g), st[:, m, 0:n], ALU.mult,
                                                 ALU.mult).then_inc(normed, 1)
        rope(k, "axial", [q[n][:, m, :] for n in range(2) for m in range(4)]
             + [kt[n][:, m, CTX:W] for n in range(2) for m in range(2)], k.rot2[:, :],
             table[:, 0, :], table[:, 1, :], sq[:, 0, :])
    pw = sb("ab_p", [P, 2, W])
    pt = sb("ab_pt", [P, 2, ST, 4 * P])
    small = sb("ab_small", [P, 2, 4])
    s_sb = sb("ab_s", [P, 2, CTX + 3 * P])
    band = sb("band", [P, 3 * P])
    sink = sb("sink", [P, 8])
    with k.stage("band_in") as (block, landed):
        @block.sync
        def _(sp):
            sp.dma_start(band[:, :], a["k_band"]).then_inc(landed, 16)
            sp.dma_start(sink[:, :], a["sink"]).then_inc(landed, 16)
            sp.wait_ge(landed, 32)
    scale = float(HD) ** -0.5

    def masked(dve, chain, u, i):
        b, s = 2 * (i % 2), s_sb[:, i % 2, :]
        chain(dve.tensor_scalar(s[:, 0:CTX], ps[:, b, 0:CTX], scale, None, ALU.mult))
        chain(dve.scalar_tensor_tensor(s[:, CTX:u["keys"]], ps[:, b + 1, 0:u["keys"] - CTX], scale,
                                       u["mask"], ALU.mult, ALU.add))

    for n, name in enumerate(("win", "glob")):
        units, groups = [], []
        for blk in range(LT):
            for g in range(2):
                lo, hi = (max(blk - 1, 0), min(blk + 1, LT - 1)) if n == 0 else (0, LT - 1)
                key_tiles = list(range(CT)) + [CT + j for j in range(lo, hi + 1)]
                nk = P * len(key_tiles)
                for i in range(4):
                    h = 4 * g + i
                    b = HD * (h % 2)
                    qs = q[n][b:b + HD, h // 2, blk * P:(blk + 1) * P]
                    kh = kt[n][b:b + HD, g, :]
                    idx = len(units)
                    u = dict(group=len(groups), keys=nk, scale=scale, at=i * P,
                             tiles=[(m * P, P) for m in range(len(key_tiles))])
                    if n == 0:
                        wl = nk - CTX
                        u["score"] = [(0, CTX, 0, [(qs, kh[:, 0:CTX])]),
                                      (1, wl, 0, [(qs, kh[:, CTX + lo * P:CTX + (hi + 1) * P])])]
                        u["span"] = s_sb[:, idx % 2, 0:nk]
                        u["dst"] = pw[:, idx % 2, 0:nk]
                        u["sink"] = sink[:, h:h + 1]
                        m0 = (lo - (blk - 1)) * P
                        u["mask"] = band[:, m0:m0 + wl]
                    else:
                        u["score"] = [(c, W // 2, 0, [(qs, kh[:, c * W // 2:(c + 1) * W // 2])])
                                      for c in range(2)]
                        u["span"] = ps[:, 2 * (idx % 2):2 * (idx % 2) + 2, 0:W // 2]
                        u["dst"] = split2(pw[:, idx % 2, :])
                    units.append(u)

                def store(dve, chain, n=n, g=g, blk=blk):
                    for b in range(2):
                        src = ps[0:HD, 6, :].rearrange("p (f b q) -> p b f q", b=2, q=P)[:, b, :, :]
                        last = dve.tensor_copy(ys[n][HD * b:HD * (b + 1), 2 * g:2 * g + 2,
                                                     blk * P:(blk + 1) * P], src)
                        if b == 0:
                            chain(last)
                    return last
                c0 = P * n + HD * g
                groups.append(dict(values=[v[:, j, c0:c0 + HD] for j in key_tiles],
                                   outs=[(0, HD, 0, 4 * P)], store=store))
        attention(k, name, units, groups, P, pw[:, :, :], pt[:, :, :, :], small[:, :, :],
                  masked if n == 0 else None)


def gated_linear(k, a, gl, w_in, hl, hc, yc):
    nc, ps = k.nc, k.ps
    D2 = range(2)

    def sb(name, shape):
        return k.sb(name, shape, stack=gl)
    q = sb("c_q", [P, 4, SEQ])
    lf = [sb(f"log_f{d}", [P, ST, 512]) for d in D2]
    kc = [sb(f"k_c{d}", [P, ST, 512]) for d in D2]
    v = sb("v_c", [P, ST, 512])
    with ExitStack() as t:
        ring = [k.sb(f"wc{i}", [P, KD, 512], stack=t) for i in range(2)]
        strips = []
        for s, (kind, c0) in enumerate((("q", 1536), ("f0", 2048), ("f1", 2560), ("v", 3072))):
            buf = ring[s % 2]
            load = [(buf[:, :, :], w_in[:, :, c0:c0 + 512])]
            if kind == "q":
                tiles = [((kind, m), [(0, 512, P, [(buf[:, i, m * P:(m + 1) * P], hl[:, i, :])
                                                   for i in range(KD)])]) for m in range(4)]
            else:
                tiles = []
                for j in range(ST):
                    src, o = (hc, j) if j < CT else (hl, j - CT)
                    tiles.append(((kind, j), [(0, 512, P, [(src[:, i, o * P:(o + 1) * P], buf[:, i, :])
                                                           for i in range(KD)])]))
            strips.append((load, tiles))
        dst = {"q": q, "f0": lf[0], "f1": lf[1], "v": v}
        linear(k, "c_in", strips, lambda dve, ch, key, bank: dve.tensor_copy(
            dst[key[0]][:, key[1], :], ps[:, bank, :]))
    with ExitStack() as t:
        forget_gates(k, a, t, q, lf, kc)
    with ExitStack() as t:
        scan(k, a, t, q, lf, kc, v, yc, hc[:, :, :].rearrange("p (h b) n -> p h (b n)", h=4))
    with ExitStack() as t:
        cg = k.sb("c_g", [P, 4, SEQ], stack=t)
        buf = k.sb("wcg", [P, KD, 512], stack=t)
        linear(k, "c_gate", [([(buf[:, :, :], w_in[:, :, 3584:4096])],
                              [(m, [(0, 512, P, [(buf[:, i, m * P:(m + 1) * P], hl[:, i, :])
                                                 for i in range(KD)])]) for m in range(4)])],
               lambda act, ch, m, bank: act.activation(cg[:, m, :], ps[:, bank, :], ACT.Silu), on="scalar")
        sq = k.sb("c_sq", [P, 4, SEQ], stack=t)
        st = k.sb("c_st", [P, 4, SEQ], stack=t)
        rms_scale(k, "c_out", [[yc[:, h, :]] for h in range(4)], float(P), k.ones[:, :], "rms", sq, st)
        with k.stage("c_gate_chain") as (block, steps):
            @block.vector
            def _(dve):
                chain = Chain(dve, steps)
                for h in range(4):
                    chain(dve.scalar_tensor_tensor(yc[:, h, :], yc[:, h, :], k.p2("gn_c"), st[:, h, :],
                                                   ALU.mult, ALU.mult))
                    chain(dve.tensor_tensor(yc[:, h, :], yc[:, h, :], cg[:, h, :], ALU.mult))


def forget_gates(k, a, t, q, lf, kc):
    nc = k.nc
    t1 = k.sb("fg_t1", [P, ST, 512], stack=t)
    t2 = k.sb("fg_t2", [P, ST, 512], stack=t)
    lb = k.sb("lb", [P, 2, 512], stack=t)
    p = k.sb("lb_p", [P, 2, 512], stack=t)
    with k.stage("lb_in", "fg_act", "fg_dve") as (block, landed, act_done, dve_done):
        @block.sync
        def _(sp):
            sp.dma_start(lb[:, :, :], a["lb"][None, :, :].to_broadcast([P, 2, 512])).then_inc(landed, 16)

        @block.scalar
        def _(act):
            chain = Chain(act, act_done)
            chain(act.activation(q[:, :, :], q[:, :, :], ACT.Silu))
            for d in range(2):
                chain(act.activation(kc[d][:, :, :], lf[d][:, :, :], ACT.Sigmoid, scale=-1.0))
            act.wait_ge(dve_done, 1)
            chain(act.activation(p[:, :, :], p[:, :, :], ACT.Exp))
            for d in range(2):
                act.wait_ge(dve_done, 7 + 6 * d)
                chain(act.activation(t1[:, :, :], t1[:, :, :], ACT.Exp, scale=-1.0))
                chain(act.activation(t1[:, :, :], t1[:, :, :], ACT.Ln, bias=k.eps("one")))
                chain(act.activation(t2[:, :, :], t2[:, :, :], ACT.Exp, scale=-1.0))
                act.wait_ge(dve_done, 8 + 6 * d)
                chain(act.activation(t2[:, :, :], t2[:, :, :], ACT.Ln, bias=k.eps("one")))

        @block.vector
        def _(dve):
            chain = Chain(dve, dve_done)
            dve.wait_ge(landed, 16)
            chain(dve.tensor_tensor(p[:, :, :], lb[:, :, :], lb[:, :, :], ALU.subtract))
            dve.wait_ge(act_done, 4)
            chain(dve.reciprocal(lb[:, :, :], p[:, :, :]))
            chain(dve.tensor_tensor(p[:, :, :], p[:, :, :], lb[:, :, :], ALU.mult))
            chain(dve.tensor_tensor(lb[:, :, :], p[:, :, :], p[:, :, :], ALU.subtract))
            chain(dve.tensor_scalar(lb[:, :, :], lb[:, :, :], 0.0, 1.0, ALU.max, ALU.min))
            for d in range(2):
                z = lf[d][:, :, :]
                wide = lambda x: x[:, d, None, :].to_broadcast([P, ST, 512])
                if d:
                    dve.wait_ge(act_done, 8)
                chain(dve.scalar_tensor_tensor(t1[:, :, :], z, -1.0, z, ALU.mult, ALU.max))
                chain(dve.tensor_scalar(t2[:, :, :], z, -44.0, None, ALU.max))
                dve.wait_ge(act_done, 7 + 4 * d)
                chain(dve.tensor_tensor(t2[:, :, :], t2[:, :, :], wide(lb), ALU.mult))
                dve.wait_ge(act_done, 8 + 4 * d)
                chain(dve.scalar_tensor_tensor(z, z, 0.0, t1[:, :, :], ALU.min, ALU.subtract))
                chain(dve.tensor_tensor(z, z, t2[:, :, :], ALU.add))
                if d == 0:
                    chain(dve.tensor_scalar(p[:, :, :], lb[:, :, :], -1.0, 1.0, ALU.mult, ALU.add))
                else:
                    chain(dve.nop())
            for d in range(2):
                chain(dve.tensor_tensor(kc[d][:, :, :], kc[d][:, :, :],
                                        p[:, d, None, :].to_broadcast([P, ST, 512]), ALU.mult))


def scan(k, a, t, q, lf, kc, v, yc, out_b):
    nc, ps = k.nc, k.ps
    D2, H = range(2), 4

    def sb(name, shape):
        return k.sb(name, shape, stack=t)
    spans = [sb(f"spans{d}", [P, 8, P]) for d in D2]
    after = [sb(f"after{d}", [P, P]) for d in D2]
    level = [sb(f"level{d}", [P, 8, P]) for d in D2]
    state = [sb(f"c_state{d}", [P, H, P]) for d in D2]
    lf_s = [sb(f"lf_s{d}", [P, 512]) for d in D2]
    k_s = [sb(f"k_s{d}", [P, 512]) for d in D2]
    v_s = [sb(f"v_s{d}", [P, 512]) for d in D2]
    k_t = [sb(f"k_t{d}", [P, H, P]) for d in D2]
    e = [sb(f"c_e{z}", [P, 8, P]) for z in D2]
    xq = [sb(f"c_xq{z}", [P, 8, P]) for z in D2]
    xk = [sb(f"c_xk{z}", [P, 7, P]) for z in D2]
    g = [sb(f"c_gm{z}", [P, 8, P]) for z in D2]
    total = sb("c_total", [P, 2 * H])
    k_out = k_s
    out = [yc, out_b]
    with k.stage("spans_in", "state_zero") as (block, landed, zeroed):
        @block.sync
        def _(sp):
            for d in D2:
                sp.dma_start(spans[d][:, :, :], a["k_spans"][d]).then_inc(landed, 16)
                sp.dma_start(after[d][:, :], a["k_after"][d]).then_inc(landed, 16)
                sp.dma_start(level[d][:, :, :], a["k_level"][d]).then_inc(landed, 16)
            sp.wait_ge(landed, 96)

        @block.vector
        def _(dve):
            for d in D2:
                dve.memset(state[d][:, :, :], 0.0).then_inc(zeroed, 1)

    def stage_tile(tiles):
        with k.stage("cut", "ahead", "turned", "ahead_exp", "weighed", "kept") as (
                block, cut, ahead, turned, ahead_exp, weighed, kept):
            @block.gpsimd
            def _(gp):
                for d in D2:
                    for dst, src in ((lf_s[d], lf[d]), (k_s[d], kc[d]), (v_s[d], v)):
                        gp.tensor_copy(dst[:, :], src[:, bass.ds(tiles[d], 1), :].rearrange(
                            "p a n -> p (a n)")).then_inc(cut, 1)

            @block.tensor
            def _(pe):
                for d in D2:
                    pe.wait_ge(cut, 3 * d + 1)
                    pe.matmul(ps[:, d, :], lhsT=after[d][:, :], rhs=lf_s[d][:, :], start=True,
                              stop=True).then_inc(ahead, 1)
                    pe.wait_ge(cut, 3 * d + 2)
                    for h in range(H):
                        last = pe.transpose(ps[:, 2 + d, h * P:(h + 1) * P],
                                            k_s[d][:, h * P:(h + 1) * P], k.ident)
                    last.then_inc(turned, 1)

            @block.scalar
            def _(act):
                for d in D2:
                    act.wait_ge(ahead, d + 1)
                    act.activation(e[d][:, 0:H, :], ps[:, d, :].rearrange("p (h n) -> p h n", h=H),
                                   ACT.Exp).then_inc(ahead_exp, 1)

            @block.vector
            def _(dve):
                for d in D2:
                    dve.wait_ge(ahead_exp, d + 1)
                    dve.wait_ge(turned, d + 1)
                    dve.tensor_tensor(k_s[d][:, :], k_s[d][:, :], e[d][:, 0:H, :].rearrange(
                        "p h n -> p (h n)"), ALU.mult).then_inc(weighed, 1)
                    dve.tensor_copy(k_t[d][:, :, :], ps[:, 2 + d, :].rearrange(
                        "p (h n) -> p h n", h=H)).then_inc(kept, 1)

    with nc.Fori(0, CT) as s:
        stage_tile([s, CT - 1 - s])
        with k.stage("made", "decayed", "ctx_chain") as (block, made, decayed, steps):
            @block.tensor
            def _(pe):
                for d in D2:
                    for h in range(H):
                        hs = slice(h * P, (h + 1) * P)
                        pe.matmul(ps[:, 4 + d, hs], lhsT=k_out[d][:, hs], rhs=v_s[d][:, hs],
                                  start=True, stop=True)
                for d in D2:
                    for h in range(H):
                        hs = slice(h * P, (h + 1) * P)
                        last = pe.matmul(ps[:, 6, 2 * (4 * d + h):2 * (4 * d + h) + 2], lhsT=lf_s[d][:, hs],
                                         rhs=k.ones[:, 0:2], start=True, stop=True)
                last.then_inc(made, 1)

            @block.scalar
            def _(act):
                act.wait_ge(made, 1)
                act.activation(total[:, :], ps[:, 6, 0:16].rearrange("p (a b) -> p a b", b=2)[:, :, 0],
                               ACT.Exp).then_inc(decayed, 1)

            @block.vector
            def _(dve):
                dve.wait_ge(decayed, 1)
                for d in D2:
                    for h in range(H):
                        dve.scalar_tensor_tensor(state[d][:, h, :], state[d][:, h, :],
                                                 total[:, 4 * d + h:4 * d + h + 1],
                                                 ps[:, 4 + d, h * P:(h + 1) * P], ALU.mult,
                                                 ALU.add).then_inc(steps, 1)

    with nc.Fori(0, LT) as s:
        lat = [s, LT - 1 - s]
        stage_tile([lat[0] + CT, lat[1] + CT])
        units = [(d, h) for d in D2 for h in range(H)]
        n_u = len(units)
        with k.stage("summed", "e_kept", "operands", "paired", "g_kept", "made", "moved", "out_kept",
                     "scan_chain") as (block, summed, e_kept, operands, paired, g_kept, made, moved,
                                       out_kept, steps):
            @block.tensor
            def _(pe):
                for i in range(n_u + 1):
                    if i < n_u:
                        d, h = units[i]
                        if i >= 2:
                            pe.wait_ge(e_kept, i - 1)
                        for c in range(2):
                            last = pe.matmul(ps[:, 2 * (i % 2) + c, :], lhsT=lf_s[d][:, h * P:(h + 1) * P],
                                             rhs=spans[d][:, 4 * c:4 * c + 4, :].rearrange("p l n -> p (l n)"),
                                             start=True, stop=True)
                        last.then_inc(summed, 1)
                    if i >= 1:
                        u = i - 1
                        d, h = units[u]
                        z = u % 2
                        hs = slice(h * P, (h + 1) * P)
                        pe.wait_ge(operands, u + 1)
                        if u >= 1:
                            pe.wait_ge(g_kept, u)
                        for l in range(8):
                            lhs, rhs = (xk[z][:, l, :], xq[z][:, l, :]) if l < 7 else (
                                k_t[d][:, h, :], q[:, h, bass.ds(lat[d] * P, P)])
                            last = pe.matmul(ps[:, 4 + l // 4, (l % 4) * P:(l % 4 + 1) * P], lhsT=lhs,
                                             rhs=rhs, start=True, stop=True)
                        last.then_inc(paired, 1)
                        pe.wait_ge(g_kept, u + 1)
                        if u >= 1:
                            pe.wait_ge(moved, u)
                            pe.wait_ge(out_kept, u)
                        o = ps[:, 6, 0:P]
                        pe.matmul(o, lhsT=state[d][:, h, :], rhs=xq[z][:, 7, :], start=True, stop=False)
                        for l in range(8):
                            pe.matmul(o, lhsT=v_s[d][:, hs], rhs=g[z][:, l, :], start=False, stop=(l == 7))
                        pe.matmul(ps[:, 7, 0:P], lhsT=k_out[d][:, hs], rhs=v_s[d][:, hs],
                                  start=True, stop=True).then_inc(made, 1)

            @block.scalar
            def _(act):
                for i in range(n_u + 1):
                    if i < n_u:
                        act.wait_ge(summed, i + 1)
                        if i >= 2:
                            act.wait_ge(moved, i - 1)
                        act.activation(e[i % 2][:, :, :].rearrange("p (b l) n -> p b (l n)", b=2),
                                       ps[:, 2 * (i % 2):2 * (i % 2) + 2, :], ACT.Exp).then_inc(e_kept, 1)
                    if i >= 1:
                        u = i - 1
                        d, h = units[u]
                        act.wait_ge(made, u + 1)
                        act.activation(out[d][:, h, bass.ds(lat[d] * P, P)], ps[:, 6, 0:P],
                                       ACT.Copy).then_inc(out_kept, 1)

            @block.vector
            def _(dve):
                chain = Chain(dve, steps)

                def operate(i):
                    d, h = units[i]
                    z = i % 2
                    dve.wait_ge(e_kept, i + 1)
                    if i >= 2:
                        dve.wait_ge(made, i - 1)
                    qd = q[:, h:h + 1, bass.ds(lat[d] * P, P)].to_broadcast([P, 8, P])
                    chain(dve.tensor_tensor(xq[z][:, :, :], e[z][:, :, :], qd, ALU.mult))
                    dve.tensor_tensor(xk[z][:, :, :], e[z][:, 0:7, :],
                                      k_t[d][:, h:h + 1, :].to_broadcast([P, 7, P]),
                                      ALU.mult).then_inc(operands, 1)

                operate(0)
                for u in range(n_u):
                    d, h = units[u]
                    z = u % 2
                    dve.wait_ge(paired, u + 1)
                    if u >= 2:
                        dve.wait_ge(made, u - 1)
                    dve.tensor_tensor(g[z][:, :, :].rearrange("p (b l) n -> p b (l n)", b=2), ps[:, 4:6, :],
                                      level[d][:, :, :].rearrange("p (b l) n -> p b (l n)", b=2),
                                      ALU.mult).then_inc(g_kept, 1)
                    if u + 1 < n_u:
                        operate(u + 1)
                    dve.wait_ge(made, u + 1)
                    end = 0 if d else P - 1
                    dve.scalar_tensor_tensor(state[d][:, h, :], state[d][:, h, :],
                                             e[z][:, 7, end:end + 1], ps[:, 7, 0:P], ALU.mult,
                                             ALU.add).then_inc(moved, 1)
    with k.stage("both_chain") as (block, steps):
        @block.vector
        def _(dve):
            dve.tensor_tensor(yc[:, :, :], yc[:, :, :], out_b[:, :, :], ALU.add).then_inc(steps, 1)


def merge(k, a, mg, w_in, hl, ys, mod, x):
    nc, ps = k.nc, k.ps
    ring = [k.sb(f"wm{i}", [P, KD, 512], stack=mg) for i in range(2)]
    gates = k.sb("gates", [P, KD, SEQ], stack=mg)
    acc = k.sb("merged", [P, KD, SEQ], stack=mg)
    tmp = k.sb("merge_tmp", [P, SEQ], stack=mg)
    for n in range(3):
        c0 = 4096 + n * D
        strips = []
        for s in range(2):
            buf = ring[s]
            strips.append(([(buf[:, :, :], w_in[:, :, c0 + s * 512:c0 + (s + 1) * 512])],
                           [(4 * s + m, [(0, SEQ, P, [(buf[:, i, m * P:(m + 1) * P], hl[:, i, :])
                                                      for i in range(KD)])]) for m in range(4)]))
        linear(k, f"gate{n}", strips, lambda act, ch, m, bank: act.activation(
            gates[:, m, :], ps[:, bank, :], ACT.Sigmoid), on="scalar")
        wb = a["w_branch_2"][0, n].rearrange("(t p) n -> p t n", p=P)
        strips = []
        for s in range(2):
            buf = ring[s]
            strips.append(([(buf[:, 0:4, :], wb[:, :, s * 512:(s + 1) * 512])],
                           [(4 * s + m, [(0, SEQ, P, [(buf[:, i, m * P:(m + 1) * P], ys[n][:, i, :])
                                                      for i in range(4)])]) for m in range(4)]))

        def evac(dve, chain, m, bank, n=n):
            if n == 0:
                return dve.tensor_tensor(acc[:, m, :], ps[:, bank, :], gates[:, m, :], ALU.mult)
            chain(dve.tensor_tensor(tmp[:, :], ps[:, bank, :], gates[:, m, :], ALU.mult))
            return dve.tensor_tensor(acc[:, m, :], acc[:, m, :], tmp[:, :], ALU.add)
        linear(k, f"up{n}", strips, evac)
    w = a["w_out_2"][0].rearrange("(t p) n -> p t n", p=P)
    strips = []
    for s in range(2):
        buf = ring[s]
        strips.append(([(buf[:, :, :], w[:, :, s * 512:(s + 1) * 512])],
                       [(4 * s + m, [(0, SEQ, P, [(buf[:, i, m * P:(m + 1) * P], acc[:, i, :])
                                                  for i in range(KD)])]) for m in range(4)]))
    linear(k, "w_out2", strips, lambda dve, ch, m, bank: dve.scalar_tensor_tensor(
        x[m], ps[:, bank, :], mod[:, 2 * KD + m, 0:1], x[m], ALU.mult, ALU.add))


def feed_forward(k, a, ff, hl, gain, mod, x):
    nc, ps = k.nc, k.ps
    up = [k.sb(f"ff_{n}", [P, FT, SEQ], stack=ff) for n in "ag"]
    w = a["w_up_2"][0].rearrange("(t p) n -> p t n", p=P)
    with ExitStack() as t:
        ring = [k.sb(f"wup{i}", [P, KD, 512], stack=t) for i in range(2)]
        pad = k.sb("ff_pad", [P, SEQ + 2], stack=t)
        with k.stage("pad_zero") as (block, zeroed):
            @block.vector
            def _(dve):
                dve.memset(pad[:, :], 0.0).then_inc(zeroed, 1)
        strips = []
        for s in range(FT // 2):
            buf = ring[s % 2]
            loads = [(buf[:, :, n * 256:(n + 1) * 256], w[:, :, n * NFF + s * 256:n * NFF + (s + 1) * 256])
                     for n in range(2)]
            strips.append((loads, [((n, 2 * s + m), [(0, SEQ, P, [
                (buf[:, i, n * 256 + m * P:n * 256 + (m + 1) * P], hl[:, i, :]) for i in range(KD)])])
                for n in range(2) for m in range(2)]))

        def evac(dve, chain, key, bank):
            n, m = key
            f = n * FT + m
            u = up[n][:, m, :]
            chain(dve.tensor_copy(pad[:, 1:SEQ + 1], ps[:, bank, :]))
            chain(dve.tensor_scalar(u, pad[:, 1:SEQ + 1], k.p2("w_dw", 2 * FT + f), k.p2("b_dw", f),
                                    ALU.mult, ALU.add))
            chain(dve.scalar_tensor_tensor(u, pad[:, 0:SEQ], k.p2("w_dw", f), u, ALU.mult, ALU.add))
            return dve.scalar_tensor_tensor(u, pad[:, 2:SEQ + 2], k.p2("w_dw", 4 * FT + f), u,
                                            ALU.mult, ALU.add)
        linear(k, "w_up", strips, evac)
    with k.stage("ff_silu", "ff_gated") as (block, silu, gated):
        @block.scalar
        def _(act):
            for m in range(FT):
                act.activation(up[1][:, m, :], up[1][:, m, :], ACT.Silu).then_inc(silu, 1)

        @block.vector
        def _(dve):
            for m in range(FT):
                dve.wait_ge(silu, m + 1)
                dve.tensor_tensor(up[0][:, m, :], up[0][:, m, :], up[1][:, m, :], ALU.mult).then_inc(gated, 1)
    wd = a["w_down_2"][0].rearrange("(t p) n -> p t n", p=P)
    with ExitStack() as t:
        ring = [k.sb(f"wdn{i}", [P, FT, P], stack=t) for i in range(2)]
        strips = [([(ring[m % 2][:, :, :], wd[:, :, m * P:(m + 1) * P])],
                   [(m, [(0, SEQ, P, [(ring[m % 2][:, i, :], up[0][:, i, :]) for i in range(FT)])])])
                  for m in range(KD)]
        linear(k, "w_down", strips, lambda dve, ch, m, bank: dve.scalar_tensor_tensor(
            x[m], ps[:, bank, :], mod[:, 5 * KD + m, 0:1], x[m], ALU.mult, ALU.add))


def finish(k, a, hl, x, sq, st):
    nc, ps = k.nc, k.ps
    modulated_norm(k, "final", x, SEQ, lambda f: k.p2("norm_final", f), None,
                   [hl[:, f, :] for f in range(KD)], sq, st)
    rows = sq
    with k.stage("o_turned", "o_kept", "o_stored") as (block, turned, kept, stored):
        @block.tensor
        def _(pe):
            for j in range(LT):
                for f in range(KD):
                    last = pe.transpose(ps[:, 2 * j + f // 4, (f % 4) * P:(f % 4 + 1) * P],
                                        hl[:, f, j * P:(j + 1) * P], k.ident)
                last.then_inc(turned, 1)

        @block.scalar
        def _(act):
            for j in range(LT):
                act.wait_ge(turned, j + 1)
                act.activation(rows[:, 2 * j:2 * j + 2, :], ps[:, 2 * j:2 * j + 2, :],
                               ACT.Copy).then_inc(kept, 1)

        @block.sync
        def _(sp):
            for j in range(LT):
                sp.wait_ge(kept, j + 1)
                sp.dma_start(a["out"][0, j * P:(j + 1) * P, :],
                             rows[:, 2 * j:2 * j + 2, :].rearrange("p a n -> p (a n)")).then_inc(stored, 16)
            sp.wait_ge(stored, 16 * LT)


def build(nc, a):
    k = Kernel(nc)
    with k.top:
        k.ps = k.top.enter_context(nc.psum_tensor("ps", [P, 8, 512], F32))
        k.cst = k.sb("cst", [P, 8])
        k.ident = k.sb("ident", [P, P])
        k.ones_d = k.sb("ones_d", [P, P])
        k.ones = k.sb("ones", [P, P])
        k.ones_h = k.sb("ones_h", [P, P])
        k.rot1 = k.sb("rot1", [P, P])
        k.rot2 = k.sb("rot2", [P, P])
        k.par1 = k.sb("par1", [P, NPAR1])
        k.par2 = k.sb("par2", [P, NPAR2])
        k.eps = lambda n: k.cst[:, EPS_COLS[n]:EPS_COLS[n] + 1]
        k.p1 = lambda n, i=0: k.par1[:, COL1[n] + i:COL1[n] + i + 1]
        k.p2 = lambda n, i=0: k.par2[:, COL2[n] + i:COL2[n] + i + 1]
        k.h = k.sb("h", [P, KD, T])
        k.v_dram = nc.dram_tensor("v_each", (LAYERS, P, RT, T), F32, kind="Internal").ap()
        k.h_rows = nc.dram_tensor("h_rows", (T, D), F32, kind="Internal").ap()
        k.y_rows = nc.dram_tensor("y_rows", (ROWS, D), F32, kind="Internal").ap()
        k.row_tok = nc.dram_tensor("row_tok", (ROWS, 1), I32, kind="Internal").ap()
        k.y_cleared = k.top.enter_context(nc.semaphore("y_cleared"))
        k.pool_dma_sems("scattered", "x_in0", "x_in1", "y0_in", "y1_in")
        with k.stage("const_landed") as (block, landed):
            @block.gpsimd
            def _(gp):
                gp.dma_start(k.y_rows.rearrange("(a p) n -> a p n", p=P),
                             a["k_zeros"][None, :, :].to_broadcast([ROWS // P, P, D])
                             ).then_inc(k.y_cleared, 16)

            @block.sync
            def _(sp):
                loads = [(k.cst, "k_cst"), (k.ones, "k_ones"), (k.ident, "k_ident"), (k.ones_d, "k_ones_d"),
                         (k.ones_h, "k_ones_h"), (k.rot1, "k_rot1"), (k.rot2, "k_rot2"),
                         (k.par2, "par2")]
                for dst, src in loads:
                    sp.dma_start(dst[:, :], a[src]).then_inc(landed, 16)
                sp.dma_start(k.row_tok, a["k_zero_rows"]).then_inc(landed, 16)
                sp.wait_ge(landed, 16 * (len(loads) + 1))
        k.ones_d, k.ones_h, k.ident = k.ones_d[:, :], k.ones_h[:, :], k.ident[:, :]
        first_block(k, a)
        second_block(k, a)


def first_block(k, a):
    nc = k.nc
    with ExitStack() as s1:
        k.cos = k.sb("cos", [P, T], stack=s1)
        k.sin = k.sb("sin", [P, T], stack=s1)
        k.keep = k.sb("keep", [P, UT], stack=s1)
        embed(k, a)
        rotary_tables(k, a)
        loop = nc.Fori(0, LAYERS)
        with loop as li:
            with ExitStack() as mix:
                k.att = k.sb("att", [P, H_A, T], stack=mix)
                k.u = k.sb("u", [P, UT, T], stack=mix)
                with ExitStack() as w:
                    k.w2 = k.sb("w2", [P, RW], stack=mix)
                    k.a2 = k.sb("a2", [P, RW], stack=mix)
                    k.g2 = k.sb("g2", [P, RW], stack=mix)
                    k.w_uq = k.sb("w_uq", [P, 2, H_A * (NOPE + ROPE)], stack=w)
                    k.w_ukv = k.sb("w_ukv", [P, H_A * (NOPE + VD)], stack=w)
                    k.mla = k.sb("mla", [P, 4, T], stack=w)
                    load_layer_params(k, a, li)
                    with ExitStack() as w2:
                        ring = [k.sb(f"win{i}", [P, KD, 512], stack=w2) for i in range(2)]
                        pad = k.sb("pad", [P, T + 2], stack=w2)
                        project_in(k, a, li, ring, pad)
                    mla(k, a)
                rwkv(k, a, li)

            moe(k, a, li)


_DIRECT = ["x", "meta_tokens", "w_in", "mla_w_uq", "mla_w_ukv", "rwkv_w2", "rwkv_a2", "rwkv_g2",
           "rwkv_v1", "rwkv_v2", "w_out", "moe_w1", "moe_w3", "moe_w2", "ctx_2", "w_mod_2", "w_in_2",
           "w_branch_2", "w_out_2", "w_up_2", "w_down_2"]


def _columns(v):
    v = np.asarray(v)
    return np.moveaxis(v.reshape(v.shape[:-1] + (-1, P)), -1, -2)


def _shape_constants():
    c = {}
    cst = np.zeros((P, 8), np.float32)
    cst[:, 0:6] = [LN_EPS, RMS_EPS, KK_EPS, GN_EPS, 1.0, np.pi / 2]
    inv = np.float32(10000.0) ** (-np.arange(0, ROPE, 2, dtype=np.float32) / np.float32(ROPE))
    cst[:, 6] = np.tile(inv.astype(np.float32), 4)
    c["k_cst"] = cst
    c["k_ones"] = np.ones((P, P), np.float32)
    c["k_ident"] = np.eye(P, dtype=np.float32)
    c["k_ones_d"] = np.full((P, P), 1.0 / D, np.float32)
    half = np.arange(P) // N_B
    c["k_ones_h"] = (half[:, None] == half[None, :]).astype(np.float32)
    rot1 = np.zeros((P, P), np.float32)
    rot2 = np.zeros((P, P), np.float32)
    for m in range(P):
        b, r = m // ROPE * ROPE, m % ROPE
        if r < 32:
            rot1[b + r + 32, m] = -1.0
        else:
            rot1[b + r - 32, m] = 1.0
        if m % 2 == 0:
            rot2[m + 1, m] = -1.0
        else:
            rot2[m - 1, m] = 1.0
    c["k_rot1"], c["k_rot2"] = rot1, rot2
    t = np.arange(P)
    low = np.zeros((P, LEVELS1, P), np.int32)
    for l in range(LEVELS1):
        s = 1 << l
        same = t[:, None] // (2 * s) == t[None, :] // (2 * s)
        low[:, l] = same & (t[:, None] // s % 2 == 1) & (t[None, :] // s % 2 == 0)
    c["k_low"] = np.ascontiguousarray(low[0:TC, :, 0:TC])
    c["k_up"] = np.ascontiguousarray(low.transpose(2, 1, 0)[0:TC, :, 0:TC])
    own = t[:, None] // PACK * PACK + np.arange(PACK)[None, :]
    for name, m in (("k_low_packed", low), ("k_up_packed", low.transpose(2, 1, 0))):
        c[name] = np.ascontiguousarray(np.take_along_axis(m[:, 0:PACKED], own[:, None, :], axis=2)[0:TC])
    block = (t[:, None] // PACK == t[None, 0:TC] // PACK)
    c["k_diag"] = np.concatenate([block, own == t[:, None]], axis=1)[0:TC].astype(np.float32)
    j, q = t[0:TC, None], t[None, 0:TC]
    tri = np.stack([j < q, j <= q, j < q, j > q, j >= q, j > q], 1).astype(np.float32)
    tri[:, [2, 5]] *= -1.0
    c["k_tri"] = np.ascontiguousarray(tri)
    reset = np.ones((P, 2, RT, TC), np.float32)
    reset[:, 0, :, 0] = 0.0
    reset[:, 1, :, TC - 1] = 0.0
    c["k_reset"] = reset
    c["k_zero_rows"] = np.zeros((ROWS, 1), np.int32)
    pos = np.arange(SEQ)
    inv2 = np.float32(10000.0) ** (-np.arange(0, 32, 2, dtype=np.float32) / np.float32(32))
    ang = np.concatenate([(pos // 64).astype(np.float32)[:, None] * inv2,
                          (pos % 64).astype(np.float32)[:, None] * inv2], axis=1)
    ang = np.tile(np.repeat(ang.T, 2, axis=0), (2, 1))
    c["k_axial"] = np.stack([np.cos(ang), np.sin(ang)], 1).astype(np.float32)
    dist = np.arange(3 * P)[None, :] - P - np.arange(P)[:, None]
    c["k_band"] = np.where(np.abs(dist) <= P, 0.0, NEG).astype(np.float32)
    s, m = t[:, None], t[None, :]
    spans, level = np.zeros((P, 8, P), np.float32), np.zeros((P, 8, P), np.float32)
    for l in range(LEVELS2):
        w = 1 << l
        mid = m // (2 * w) * 2 * w + w
        spans[:, l] = np.where(m >= mid, (s >= mid) & (s <= m), (s > m) & (s < mid))
        level[:, l] = (s // (2 * w) == m // (2 * w)) & (s // w % 2 == 0) & (m // w % 2 == 1)
    spans[:, 7] = s <= m
    level[:, 7] = s == m
    c["k_spans"] = np.stack([spans, spans[::-1, :, ::-1]])
    c["k_level"] = np.stack([level, level[::-1, :, ::-1]])
    after = (s > m).astype(np.float32)
    c["k_after"] = np.stack([after, after[::-1, ::-1]])
    c["k_zeros"] = np.zeros((P, D), np.float32)
    c["k_iota"] = np.tile(np.arange(64, dtype=np.float32), (TC, 1))
    c["k_tok"] = (np.arange(NC1)[None, :] * TC + np.arange(TC)[:, None]).astype(np.int32)
    return c


def kernel(**inputs):
    from concourse import bacc
    from concourse.bass_utils import run_bass_kernel_spmd

    x = {n: np.asarray(v) for n, v in inputs.items()}
    arrays = {n: x[n] for n in _DIRECT}
    arrays["positions"] = x["positions"]
    names1 = {"q_norm": "mla_q_norm", "kv_norm": "mla_kv_norm", "out_norm": "mla_out_norm",
              "mu_prev": "rwkv_mu_prev", "mu_next": "rwkv_mu_next", "w0": "rwkv_w0", "a0": "rwkv_a0",
              "k_k": "rwkv_k_k", "k_a": "rwkv_k_a", "r_k": "rwkv_r_k", "gn_g": "rwkv_gn_g",
              "gn_b": "rwkv_gn_b", "ln1_g": "ln1_g", "ln1_b": "ln1_b", "ln2_g": "ln2_g",
              "ln2_b": "ln2_b"}
    arrays["par1"] = np.concatenate(
        [_columns(x[names1[n]].reshape(LAYERS, -1)) for n, _ in PARAMS1], axis=2)
    two = lambda v: np.concatenate([v, v], axis=-1)
    flat = {"v0": x["rwkv_v0"][0], "emb_g": x["emb_ln_g"], "emb_b": x["emb_ln_b"], "c": x["c_2"][0],
            "c_ctx": x["c_ctx_2"], "b_mod": x["b_mod_2"][0], "norm_mix": x["norm_mix_2"][0],
            "norm_ffn": x["norm_ffn_2"][0], "qn": two(x["qn_b_2"][0]), "kn": two(x["kn_b_2"][0]),
            "gn_c": x["gn_c_2"][0], "w_dw": x["w_dw_2"][0].reshape(-1), "b_dw": x["b_dw_2"][0],
            "norm_final": x["norm_final_2"]}
    arrays["par2"] = np.concatenate([_columns(flat[n]) for n, _ in PARAMS2], axis=1)
    arrays["sink"] = np.broadcast_to(x["sink_a_2"], (P, 8))
    arrays["lb"] = np.concatenate([x["lb_fwd_2"], x["lb_bwd_2"]], axis=0)
    arrays["router"] = np.concatenate([x["moe_w_group"], x["moe_w_expert"]], axis=2)
    arrays["router_b"] = np.concatenate([x["moe_b_group"], x["moe_b_expert"]], axis=1)
    arrays.update(_shape_constants())

    nc = bacc.Bacc("TRN2", target_bir_lowering=False, num_devices=1)
    held, a = {}, {}
    for name, value in arrays.items():
        value = np.ascontiguousarray(value)
        held[f"in_{name}"] = value
        a[name] = nc.dram_tensor(f"in_{name}", value.shape, mybir.dt.from_np(value.dtype),
                                 kind="ExternalInput").ap()
    a["out"] = nc.dram_tensor("out_0", (1, SEQ, D), F32, kind="ExternalOutput").ap()
    build(nc, a)
    r = run_bass_kernel_spmd(nc, [held], core_ids=[0])
    return r.results[0]["out_0"]
```
